# Optimizing a Trainium2 kernel written in Bass

```python
import math
import jax
import jax.numpy as jnp
from jax import lax
import numpy as np

'''Hybrid autoregressive decoder trunk (DEPTH layers, all mixers causal).
Each layer: RMSNorm -> ONE combined input projection whose columns are partitioned among
four parallel token mixers (mLSTM matrix memory, gated short convolution, Mamba-2 SSD,
stick-breaking attention) plus four per-channel branch gates -> each branch lifted to
D_MODEL by its row-block of w_lift -> sigmoid-gated per-channel sum -> ONE output
projection -> residual add; then RMSNorm -> gated MLP with a causal depthwise width-3
convolution between up-projection and activation -> residual add. Final RMSNorm.
Input  x: (BATCH, SEQ, D_MODEL) float32.
Output  : (BATCH, SEQ, D_MODEL).
'''

D_MODEL = 1024
BATCH = 1
SEQ = 512
DEPTH = 1

A_HEADS = 4
A_QK_DIM = 64
A_V_DIM = 128
A_WIDTH = A_HEADS * A_V_DIM
B_WIDTH = 512
B_CONV = 3
C_HEADDIM = 64
C_WIDTH = 512
C_HEADS = C_WIDTH // C_HEADDIM
C_GROUPS = 2
C_HPG = C_HEADS // C_GROUPS
C_STATE = 128
C_CONV = 4
C_CONV_CH = C_WIDTH + 2 * C_GROUPS * C_STATE
DT_MIN = 1e-3
DT_MAX = 1e-1
D_HEADS = 4
D_HEAD_DIM = 128
D_WIDTH = D_HEADS * D_HEAD_DIM
Q_BLOCK = 128
N_BRANCH = 4
BRANCH_WIDTH = 512
CHUNK = 64
D_FF = 2816
FFN_CONV = 3
EPS = 1e-6
NEG = -1e30

SPLITS = (A_HEADS * A_QK_DIM, A_HEADS * A_QK_DIM, A_WIDTH, A_WIDTH, A_HEADS, A_HEADS,
          B_WIDTH, B_WIDTH, B_WIDTH,
          C_WIDTH, C_CONV_CH, C_HEADS,
          D_WIDTH, D_WIDTH, D_WIDTH,
          N_BRANCH * D_MODEL)
P_IN = sum(SPLITS)
SPLIT_POINTS = tuple(int(v) for v in np.cumsum(SPLITS)[:-1])

kernel_name = 'hybrid_gated_mlstm_shortconv_ssd_stickbreak'

def rmsnorm(x, g):
    xf = x.astype(jnp.float32)
    y = xf * lax.rsqrt(jnp.mean(xf * xf, axis=-1, keepdims=True) + EPS)
    return (y * g.astype(jnp.float32)).astype(x.dtype)

def causal_dwconv(x, w):
    K = w.shape[0]
    S = x.shape[1]
    xp = jnp.pad(x, ((0, 0), (K - 1, 0), (0, 0)))
    out = xp[:, 0:S] * w[0]
    for j in range(1, K):
        out = out + xp[:, j:j + S] * w[j]
    return out

def to_chunks(t):
    Bn, S = t.shape[0], t.shape[1]
    return jnp.moveaxis(t.reshape(Bn, S // CHUNK, CHUNK, *t.shape[2:]), 1, 0)

def from_chunks(t):
    nc, Bn, L = t.shape[0], t.shape[1], t.shape[2]
    return jnp.moveaxis(t, 0, 1).reshape(Bn, nc * L, *t.shape[3:])

def mlstm(q, k, v, o, ig, fg, norm_g):
    f32 = jnp.float32
    Bn, S = q.shape[0], q.shape[1]
    q = q.reshape(Bn, S, A_HEADS, A_QK_DIM).astype(f32) * (A_QK_DIM ** -0.5)
    k = k.reshape(Bn, S, A_HEADS, A_QK_DIM).astype(f32)
    v = v.reshape(Bn, S, A_HEADS, A_V_DIM).astype(f32)
    ig = ig.astype(f32)
    lf = jax.nn.log_sigmoid(fg.astype(f32))
    qc = jnp.swapaxes(to_chunks(q), 2, 3)
    kc = jnp.swapaxes(to_chunks(k), 2, 3)
    vc = jnp.swapaxes(to_chunks(v), 2, 3)
    igc = jnp.swapaxes(to_chunks(ig), 2, 3)
    lfc = jnp.swapaxes(to_chunks(lf), 2, 3)
    tri = jnp.tril(jnp.ones((CHUNK, CHUNK), dtype=bool))

    def step(carry, xs):
        C, n, m = carry
        qx, kx, vx, ix, fx = xs
        b = jnp.cumsum(fx, axis=-1)
        logD = jnp.where(tri, b[..., :, None] - b[..., None, :] + ix[..., None, :], NEG)
        inter = b + m[..., None]
        m_t = jnp.maximum(inter, jnp.max(logD, axis=-1))
        Dm = jnp.exp(logD - m_t[..., None])
        inter_s = jnp.exp(inter - m_t)
        Sm = jnp.einsum('bhtk,bhsk->bhts', qx, kx) * Dm
        num = jnp.einsum('bhts,bhsv->bhtv', Sm, vx) + inter_s[..., None] * jnp.einsum('bhtk,bhkv->bhtv', qx, C)
        den = jnp.sum(Sm, axis=-1) + inter_s * jnp.einsum('bhtk,bhk->bht', qx, n)
        h = num / jnp.maximum(jnp.abs(den), jnp.exp(-m_t))[..., None]
        bL = b[..., -1]
        logw = bL[..., None] - b + ix
        m_new = jnp.maximum(bL + m, jnp.max(logw, axis=-1))
        w = jnp.exp(logw - m_new[..., None])
        sc = jnp.exp(bL + m - m_new)
        C = sc[..., None, None] * C + jnp.einsum('bhs,bhsk,bhsv->bhkv', w, kx, vx)
        n = sc[..., None] * n + jnp.einsum('bhs,bhsk->bhk', w, kx)
        return (C, n, m_new), h

    init = (jnp.zeros((Bn, A_HEADS, A_QK_DIM, A_V_DIM), f32),
            jnp.zeros((Bn, A_HEADS, A_QK_DIM), f32),
            jnp.zeros((Bn, A_HEADS), f32))
    _, h = lax.scan(step, init, (qc, kc, vc, igc, lfc))
    h = from_chunks(jnp.swapaxes(h, 2, 3))
    h = h * lax.rsqrt(jnp.mean(h * h, axis=-1, keepdims=True) + EPS)
    h = h.reshape(Bn, S, A_WIDTH) * norm_g.astype(f32)
    return (jax.nn.sigmoid(o.astype(f32)) * h).astype(o.dtype)

def short_conv_mixer(bg, cg, xb, conv_w):
    return bg * causal_dwconv(cg * xb, conv_w)

def ssd_scan(x, dt, A, Bm, Cm):
    f32 = jnp.float32
    Bn = x.shape[0]
    tri = jnp.tril(jnp.ones((CHUNK, CHUNK), dtype=bool))

    def step(h, xs):
        xx, dd, bb, cc = xs
        a = jnp.cumsum(dd * A, axis=1)
        seg = a[:, :, None] - a[:, None, :]
        Ldec = jnp.exp(jnp.where(tri[:, :, None, None], seg, NEG))
        CB = jnp.einsum('btgn,bsgn->btsg', cc, bb)
        y_diag = jnp.einsum('btsg,btsgh,bsgh,bsghp->btghp', CB, Ldec, dd, xx)
        y_off = jnp.einsum('btgn,bghpn->btghp', cc, h) * jnp.exp(a)[..., None]
        a_last = a[:, -1]
        wdec = jnp.exp(a_last[:, None] - a) * dd
        h = h * jnp.exp(a_last)[..., None, None] + jnp.einsum('bsgn,bsgh,bsghp->bghpn', bb, wdec, xx)
        return h, y_diag + y_off

    h0 = jnp.zeros((Bn, C_GROUPS, C_HPG, C_HEADDIM, C_STATE), f32)
    _, y = lax.scan(step, h0, (to_chunks(x), to_chunks(dt), to_chunks(Bm), to_chunks(Cm)))
    return from_chunks(y)

def mamba2_mixer(z, xbc, dt_raw, conv_w, conv_b, dt_bias, a_log, d_skip, norm_g):
    f32 = jnp.float32
    Bn, S = z.shape[0], z.shape[1]
    xbc = jax.nn.silu(causal_dwconv(xbc, conv_w) + conv_b).astype(f32)
    xs = xbc[..., :C_WIDTH].reshape(Bn, S, C_GROUPS, C_HPG, C_HEADDIM)
    Bm = xbc[..., C_WIDTH:C_WIDTH + C_GROUPS * C_STATE].reshape(Bn, S, C_GROUPS, C_STATE)
    Cm = xbc[..., C_WIDTH + C_GROUPS * C_STATE:].reshape(Bn, S, C_GROUPS, C_STATE)
    dt = jax.nn.softplus(dt_raw.astype(f32) + dt_bias.astype(f32)).reshape(Bn, S, C_GROUPS, C_HPG)
    A = -jnp.exp(a_log.astype(f32)).reshape(C_GROUPS, C_HPG)
    y = ssd_scan(xs, dt, A, Bm, Cm)
    y = y + d_skip.astype(f32).reshape(C_GROUPS, C_HPG)[..., None] * xs
    y = y.reshape(Bn, S, C_WIDTH) * jax.nn.silu(z.astype(f32))
    return rmsnorm(y, norm_g).astype(z.dtype)

def stick_breaking_attention(q, k, v):
    f32 = jnp.float32
    Bn, S = q.shape[0], q.shape[1]
    def heads(t):
        return t.reshape(Bn, S, D_HEADS, D_HEAD_DIM).transpose(0, 2, 1, 3).astype(f32)
    qh = heads(q) * (D_HEAD_DIM ** -0.5)
    kh = heads(k)
    vh = heads(v)
    nb = S // Q_BLOCK
    qb = qh.reshape(Bn, D_HEADS, nb, Q_BLOCK, D_HEAD_DIM).transpose(2, 0, 1, 3, 4)
    key_pos = jnp.arange(S)

    def block(args):
        qblk, start = args
        z = jnp.einsum('bhtd,bhsd->bhts', qblk, kh)
        t_pos = start + jnp.arange(Q_BLOCK)
        mask = key_pos[None, :] < t_pos[:, None]
        log_rest = jnp.where(mask, jax.nn.log_sigmoid(-z), 0.0)
        shifted = jnp.concatenate([log_rest[..., 1:], jnp.zeros_like(log_rest[..., :1])], axis=-1)
        R = lax.cumsum(shifted, axis=3, reverse=True)
        A = jnp.where(mask, jnp.exp(jax.nn.log_sigmoid(z) + R), 0.0)
        return jnp.einsum('bhts,bhsd->bhtd', A, vh)

    starts = jnp.arange(nb) * Q_BLOCK
    out = lax.map(block, (qb, starts))
    out = out.transpose(1, 0, 3, 2, 4).reshape(Bn, S, D_WIDTH)
    return out.astype(q.dtype)

def conv_glu_mlp(x, w_up, conv_w, conv_b, w_down):
    h = causal_dwconv(x @ w_up, conv_w) + conv_b
    g, u = jnp.split(h, 2, axis=-1)
    return (jax.nn.silu(g) * u) @ w_down

def setup_inputs(seed: int = 0) -> dict:
    key = jax.random.key(seed)
    ks = jax.random.split(key, 22)
    f32 = jnp.float32

    def nrm(k, shape, scale):
        return jax.random.normal(k, shape, f32) * scale

    def gain(k, shape):
        return 1.0 + 0.1 * jax.random.normal(k, shape, f32)

    dt0 = jnp.exp(jax.random.uniform(ks[9], (DEPTH, C_HEADS), f32, math.log(DT_MIN), math.log(DT_MAX)))
    return {
        'x': nrm(ks[0], (BATCH, SEQ, D_MODEL), 1.0),
        'mix_norm_g': gain(ks[1], (DEPTH, D_MODEL)),
        'w_in': nrm(ks[2], (DEPTH, D_MODEL, P_IN), D_MODEL ** -0.5),
        'a_igate_b': nrm(ks[3], (DEPTH, A_HEADS), 0.1),
        'a_fgate_b': jnp.linspace(3.0, 6.0, A_HEADS, dtype=f32)[None, :] + nrm(ks[4], (DEPTH, A_HEADS), 0.1),
        'a_norm_g': gain(ks[5], (DEPTH, A_WIDTH)),
        'b_conv_w': nrm(ks[6], (DEPTH, B_CONV, B_WIDTH), B_CONV ** -0.5),
        'c_conv_w': nrm(ks[7], (DEPTH, C_CONV, C_CONV_CH), C_CONV ** -0.5),
        'c_conv_b': nrm(ks[8], (DEPTH, C_CONV_CH), 0.02),
        'c_dt_bias': jnp.log(jnp.expm1(dt0)),
        'c_a_log': jnp.log(jax.random.uniform(ks[10], (DEPTH, C_HEADS), f32, 1.0, 16.0)),
        'c_d_skip': gain(ks[11], (DEPTH, C_HEADS)),
        'c_norm_g': gain(ks[12], (DEPTH, C_WIDTH)),
        'w_lift': nrm(ks[13], (DEPTH, N_BRANCH, BRANCH_WIDTH, D_MODEL), BRANCH_WIDTH ** -0.5),
        'w_out': nrm(ks[14], (DEPTH, D_MODEL, D_MODEL), D_MODEL ** -0.5),
        'ffn_norm_g': gain(ks[15], (DEPTH, D_MODEL)),
        'w_up': nrm(ks[16], (DEPTH, D_MODEL, 2 * D_FF), D_MODEL ** -0.5),
        'ffn_conv_w': nrm(ks[17], (DEPTH, FFN_CONV, 2 * D_FF), FFN_CONV ** -0.5),
        'ffn_conv_b': nrm(ks[18], (DEPTH, 2 * D_FF), 0.02),
        'w_down': nrm(ks[19], (DEPTH, D_FF, D_MODEL), D_FF ** -0.5),
        'final_norm_g': gain(ks[20], (D_MODEL,)),
    }

def reference(x, mix_norm_g, w_in, a_igate_b, a_fgate_b, a_norm_g, b_conv_w, c_conv_w, c_conv_b,
              c_dt_bias, c_a_log, c_d_skip, c_norm_g, w_lift, w_out, ffn_norm_g, w_up,
              ffn_conv_w, ffn_conv_b, w_down, final_norm_g):
    Bn, S = x.shape[0], x.shape[1]
    for l in range(DEPTH):
        xn = rmsnorm(x, mix_norm_g[l])
        p = xn @ w_in[l]
        (aq, ak, av, ao, ai, af, bb, bc, bx, cz, cxbc, cdt,
         sq, sk, sv, gates) = jnp.split(p, SPLIT_POINTS, axis=-1)
        ya = mlstm(aq, ak, av, ao, ai + a_igate_b[l], af + a_fgate_b[l], a_norm_g[l])
        yb = short_conv_mixer(bb, bc, bx, b_conv_w[l])
        yc = mamba2_mixer(cz, cxbc, cdt, c_conv_w[l], c_conv_b[l], c_dt_bias[l], c_a_log[l],
                          c_d_skip[l], c_norm_g[l])
        yd = stick_breaking_attention(sq, sk, sv)
        ycat = jnp.stack([ya, yb, yc, yd], axis=2)
        lifted = jnp.einsum('bsie,ied->bsid', ycat, w_lift[l])
        g = jax.nn.sigmoid(gates.reshape(Bn, S, N_BRANCH, D_MODEL))
        merged = jnp.einsum('bsid,bsid->bsd', g, lifted)
        x = x + merged @ w_out[l]
        x = x + conv_glu_mlp(rmsnorm(x, ffn_norm_g[l]), w_up[l], ffn_conv_w[l], ffn_conv_b[l], w_down[l])
    return rmsnorm(x, final_norm_g)


_drawn_inputs = setup_inputs


def setup_inputs(seed=0):
    import zlib

    import numpy as np

    out = dict(_drawn_inputs(seed))
    spreads = {}
    factors = {'a_igate_b': 8.0, 'c_conv_b': 5.022, 'ffn_conv_b': 4.88}
    for name, (base, spread) in spreads.items():
        noise = np.random.default_rng([zlib.crc32(name.encode()), seed]).standard_normal(out[name].shape)
        drawn = base * np.exp(spread * noise) if base else spread * noise
        out[name] = jnp.asarray(drawn.astype(out[name].dtype))
    for name, factor in factors.items():
        out[name] = (out[name] * factor).astype(out[name].dtype)
    return out
```

```python
from contextlib import ExitStack

import numpy as np
import concourse.bass as bass
from concourse import mybir

ALU = mybir.AluOpType
ACT = mybir.ActivationFunctionType
F32 = mybir.dt.float32
F32R = mybir.dt.float32r

P = 128
T = 512
D = 1024
KD = D // P
FF = 2816
NFF = FF // P
NB = T // P
BLK_W = [T - P * j for j in range(NB)]
BLK_O = [sum(BLK_W[:j]) for j in range(NB)]
PACK = sum(BLK_W)
EPS = 1e-6
NEG = -1e30
A_HEADS, C_HEADS, D_HEADS = 4, 8, 4
A_SCALE = 64 ** -0.5
D_SCALE = 128 ** -0.5

U_DQ, U_DK, U_DV = 0, 4, 8
U_SMALL = 12
U_AQ, U_AK, U_AV, U_AO = 13, 15, 17, 21
U_Z, U_XBC = 25, 29
U_GL_D, U_B, U_GL_A, U_GL_B, U_GL_C = 37, 49, 61, 73, 85
U_OUT = 97
U_UP = U_OUT + KD
U_DOWN = U_UP + 2 * NFF
N_STREAM = U_DOWN
DOWN_K = [6, 6, 5, 5]
DOWN_K0 = [0, 6, 12, 17]
N_UNITS = U_DOWN + 4 * KD
RING = 4
GL = {U_GL_D: 0, U_GL_A: 1, U_GL_B: 0, U_GL_C: 1}
D_AT = [12 + 4 * h for h in range(D_HEADS)]
A_AT = [29 + 5 * h for h in range(A_HEADS)]
C_AT = [53 + 2 * h for h in range(C_HEADS)]

V_MIX, V_FFN, V_FIN, V_AG = 0, 8, 16, 24
V_BCW, V_CCW, V_CCB, V_CNG, V_DSK = 28, 40, 72, 80, 84
V_FCW = 88
N_VEC = V_FCW + 4 * 2 * NFF


def front_tiles():
    made = {}
    for u in range(U_OUT):
        n, who = 1, "dve"
        if u in (U_DV, U_DV + 2, U_AV, U_AV + 2):
            n = 0
        elif u in (U_DV + 1, U_DV + 3, U_AV + 1, U_AV + 3):
            n = 2
        elif U_AO <= u < U_XBC:
            who = "act"
        for g in GL:
            if g <= u < g + 12:
                n, who = (2, "dve") if (u - g) % 3 == 2 else (1, "act")
        made[u] = (n, who)
    return made


def build(nc, w_stream, w_down, xT, vecs, rowsm, outT):
    made = front_tiles()
    first_tile, order = {}, []
    counts = {"dve": 0, "act": 0}
    for u in range(U_OUT):
        first_tile[u] = len(order)
        n, who = made[u]
        for _ in range(n):
            counts[who] += 1
            order.append((who, counts[who]))
    TILES0, DVE0, ACT0 = len(order), counts["dve"], counts["act"]

    ctx = ExitStack()
    base = 16512

    def at(name, shape, dt, offset):
        return nc.alloc_sbuf_tensor_at(name, shape, dt, offset=offset)

    class Map:

        def __init__(self, offset):
            self.at = offset

        def put(self, name, shape, dt=F32):
            size = 4 * int(np.prod(shape[1:]))
            t = at(name, shape, dt, self.at)
            self.at += (size + 31) // 32 * 32
            return t

    m = Map(base)
    raw = m.put("raw", [P, RING, 1024])
    w_hi = m.put("w_hi", [P, RING, 1024], F32R)
    w_lo = m.put("w_lo", [P, RING, 1024], F32R)
    xn_hi = m.put("xn_hi", [P, KD, T], F32R)
    xn_lo = m.put("xn_lo", [P, KD, T], F32R)
    ones = m.put("ones", [P, P])
    ident = m.put("ident", [P, P])
    tri = m.put("tri", [P, P])
    causal = m.put("causal", [P, P])
    colT = m.put("colT", [P, NB, P])
    vec = m.put("vec", [P, N_VEC])
    fcw = vec[:, V_FCW:N_VEC].rearrange("p (t c) -> p t c", c=4)
    rsm = m.put("rsm", [40, 4])
    cst = m.put("cst", [P, 4])
    END_CONST = m.at
    y_hi = m.put("y_hi", [P, 2, 4, T], F32R)
    y_lo = m.put("y_lo", [P, 2, 4, T], F32R)
    G0 = m.at
    merged = m.put("merged", [P, KD, T])
    gate = m.put("gate", [P, 2, 2, T])
    t0 = m.put("t0", [P, PACK])
    t1 = m.put("t1", [P, PACK])
    A0 = m.at
    aq = m.put("aq", [P, 2, T])
    ak = m.put("ak", [P, 2, T])
    av = m.put("av", [P, NB, T])
    ao = m.put("ao", [P, 4, T])
    C0 = m.at
    zy = m.put("zy", [P, 4, T])
    xbc = m.put("xbc", [P, 8, T])
    stg = m.put("stg", [P, 2, T])
    nmb = m.put("nmb", [P, T])
    enb = m.put("enb", [P, T])
    assert m.at <= 229344, m.at
    g = Map(G0)
    dq, dk, dv = (g.put(n, [P, 4, T]) for n in ("dq", "dk", "dv"))
    x_in = at("x_in", [P, KD, T], F32, G0)
    y1 = END_CONST + 4 * 4 * T
    g = Map(y1)
    negm = g.put("negm", [P, T])
    g_sp = g.put("g_sp", [40, T])
    g_ab = g.put("g_ab", [40, T])
    g_x = g.put("g_x", [40, T])
    y1 = END_CONST + 4 * 2 * 4 * T + 4 * 4 * T
    g = Map(y1)
    g_row = g.put("g_row", [P, T])
    g_nm = g.put("g_nm", [4, 2, T])
    g_i = g.put("g_i", [4, T])
    a_run = at("a_run", [40, PACK], F32, C0 + 4 * 4 * T)
    g_one = at("g_one", [40, T], F32, C0 + 4 * 4 * T + 4 * PACK)
    g_b = at("g_b", [40, T], F32, C0 + 4 * 4 * T + 4 * PACK + 4 * T)
    g = Map(A0)
    xdt = g.put("xdt", [P, NB, T])
    cbm = g.put("cbm", [P, PACK])
    abc = g.put("abc", [P, PACK])
    assert g.at <= C0
    g = Map(END_CONST)
    h_hi = g.put("h_hi", [P, NFF, T], F32R)
    h_lo = g.put("h_lo", [P, NFF, T], F32R)
    assert g.at <= C0
    g = Map(C0)
    x1 = g.put("x1", [P, KD, T])
    f_cv = g.put("f_cv", [P, 2, 2, T])
    f_si = g.put("f_si", [P, T])
    f_sq = g.put("f_sq", [P, T])
    f_ac = g.put("f_ac", [P, T])
    f_rs = g.put("f_rs", [P, T])
    assert g.at <= 229344

    GB = [ctx.enter_context(nc.psum_tensor(f"gb{i}", [P, T], F32)) for i in range(4)]
    X = [ctx.enter_context(nc.psum_tensor(f"xb{i}", [P, T], F32)) for i in range(4)]
    scr = nc.dram_tensor("scr_rows", [8, T], F32).ap()
    scr_a = nc.dram_tensor("scr_a", [8, PACK], F32).ap()

    names = """raw0 raw1 raw2 raw3 x_loaded vec_loaded built hi_ready lo_ready unit_done
        psum_read_dve psum_read_act act_own dve_own
        n1_sum_in n1_sqr n1_sum n1_rstd n1_xn n1_hi xn_ready
        gates_made merged_put merged_hi merged_ready
        d_scores d_masked d_soft_in d_soft d_suffix d_expo d_weights d_out d_hi d_lo
        g_log g_rows g_en g_trans g_cols rows_out a_out
        a_nm a_en a_arg a_dec a_scores a_w a_numden a_h a_sq a_sum a_rstd a_y a_hi a_lo
        b_hi b_lo x_tap z_made
        c_trans c_xdt c_cb c_cbm c_abc c_arg c_dec c_w c_y c_z c_sq c_acc c_sum c_rstd c_fin c_hi c_lo
        x_again wo_sq wo_acc n2_sum n2_rstd n2_xn n2_hi n2_ready
        f_tap f_tap1 f_silu f_h f_hi f_lo o_sq o_acc o_sum o_rstd o_fin out_stored""".split()
    S = {n: ctx.enter_context(nc.semaphore(n)) for n in names}
    block = ctx.enter_context(nc.Block())

    def blk(j):
        return slice(BLK_O[j], BLK_O[j] + BLK_W[j])

    def diag(j):
        return slice(BLK_O[j], BLK_O[j] + P)

    @block.sync
    def _(sp):
        for k in range(KD):
            sp.dma_start(x_in[:, k, :], xT[:, k, :]).then_inc(S["x_loaded"], 16)
            if k == 0:
                sp.dma_start(vec[:], vecs).then_inc(S["vec_loaded"], 16)
                sp.dma_start(rsm[:], rowsm).then_inc(S["vec_loaded"], 16)
            if k % 2 == 1:
                r = k // 2
                sp.dma_start(raw[:, r, :], w_stream[r]).then_inc(S[f"raw{r}"], 16)
        with sp.Fori(1, U_DOWN // RING) as i:
            for r in range(RING):
                sp.wait_ge(S["lo_ready"], RING * i - RING + r + 1)
                sp.dma_start(raw[:, r, :], w_stream[RING * i + r]).then_inc(S[f"raw{r}"], 16)
        r = 0
        sp.wait_ge(S["lo_ready"], U_DOWN - RING)
        sp.dma_start(raw[:, r, :], w_stream[U_DOWN - 1]).then_inc(S[f"raw{r}"], 16)
        for q in range(4 * KD):
            u = U_DOWN + q
            sp.wait_ge(S["lo_ready"], u - RING + 1)
            n = DOWN_K[q % 4] * P
            sp.dma_start(raw[:, u % RING, 0:n], w_down[q][:, 0:n]).then_inc(S[f"raw{u % RING}"], 16)
        for k in range(KD):
            sp.wait_ge(S["o_fin"], k + 1)
            sp.dma_start(outT[:, k, :], x1[:, k, :]).then_inc(S["out_stored"], 16)
        sp.wait_ge(S["out_stored"], 16 * KD)

    @block.gpsimd
    def _(pool):
        n = 0

        def made_const(ins):
            nonlocal n
            ins.then_inc(S["built"], 1)
            n += 1

        made_const(pool.memset(ones[:], 1.0))
        made_const(pool.memset(cst[:, 0:1], 1.0))
        made_const(pool.memset(cst[:, 1:2], EPS))
        made_const(pool.memset(ident[:], 0.0))
        made_const(pool.memset(tri[:], 1.0))
        made_const(pool.memset(causal[:], 1.0))
        made_const(pool.memset(negm[:], 0.0))
        made_const(pool.memset(g_x[:], 0.0))
        made_const(pool.memset(g_row[:], 0.0))
        made_const(pool.memset(g_one[:], 1.0))
        pool.wait_ge(S["built"], n)
        made_const(pool.affine_select(out=ident[:], in_=ident[:], compare_op=ALU.not_equal, fill=1.0,
                                      base=0, pattern=[[-1, P]], channel_multiplier=1))
        made_const(pool.affine_select(out=tri[:], in_=tri[:], compare_op=ALU.is_ge, fill=0.0,
                                      base=0, pattern=[[-1, P]], channel_multiplier=1))
        made_const(pool.affine_select(out=causal[:], in_=causal[:], compare_op=ALU.is_ge, fill=0.0,
                                      base=0, pattern=[[1, P]], channel_multiplier=-1))
        made_const(pool.affine_select(out=negm[:], in_=negm[:], compare_op=ALU.is_ge, fill=NEG,
                                      base=-1, pattern=[[1, T]], channel_multiplier=-1))
        pool.wait_ge(S["g_rows"], 1)
        pool.wait_ge(S["g_en"], 1)
        pool.dma_start(scr.rearrange("(w h) t -> h w t", h=4), g_nm[:, :, :]).then_inc(S["rows_out"], 16)
        pool.dma_start(scr_a, a_run[32:40, :]).then_inc(S["a_out"], 16)
        pool.wait_ge(S["rows_out"], 16)
        pool.wait_ge(S["a_out"], 16)
        for h in range(A_HEADS):
            if h:
                pool.wait_ge(S["a_arg"], 4 * h)
            pool.dma_start(nmb[:], scr[h:h + 1, :].to_broadcast([P, T])).then_inc(S["a_nm"], 16)
            if h:
                pool.wait_ge(S["a_h"], h)
            pool.dma_start(enb[:], scr[4 + h:5 + h, :].to_broadcast([P, T])).then_inc(S["a_en"], 16)
        for h in range(C_HEADS):
            if h:
                pool.wait_ge(S["c_arg"], 4 * h)
            else:
                pool.wait_ge(S["a_y"], 2 * A_HEADS)
            pool.dma_start(abc[:], scr_a[h:h + 1, :].to_broadcast([P, PACK])).then_inc(S["c_abc"], 16)
        pool.wait_ge(S["c_lo"], 4)
        pool.dma_start(x1[:], xT).then_inc(S["x_again"], 16)
        pool.wait_ge(S["x_again"], 16)

    @block.tensor
    def _(pe):
        def gemm(out, r, c0, rhs, ks, kk0=0, kstep=1, first=True, last_=True):
            for n, k in enumerate(ks):
                lo, hi = c0 + n * P, c0 + n * P + P
                for q, (w, x) in enumerate(((w_hi, 0), (w_hi, 1), (w_lo, 0))):
                    ins = pe.matmul(out, w[:, r, lo:hi], rhs(k)[x], start=(first and n == 0 and q == 0),
                                    stop=(last_ and n == len(ks) - 1 and q == 2))
            return ins

        def xn(k):
            return xn_hi[:, k, :], xn_lo[:, k, :]

        def bank_free(o):
            if o >= 4:
                who, n = order[o - 4]
                pe.wait_ge(S[f"psum_read_{who}"], n)

        def unit(u):
            o = first_tile[u]
            n = made[u][0]
            pe.wait_ge(S["lo_ready"], u + 1)
            if n == 0:
                return
            for q in range(n):
                bank_free(o + q)
            if U_DV < u < U_DV + 4 or U_AV < u < U_AV + 4:
                for tb in range(NB):
                    out = GB[(o + tb // 2) % 4][:, 256 * (tb % 2):256 * (tb % 2) + 256]
                    for k in range(KD):
                        r = (u - 1 + k // 4) % RING
                        c = (k % 4) * 256
                        for q, (x, w) in enumerate(((xn_hi, w_hi), (xn_lo, w_hi), (xn_hi, w_lo))):
                            ins = pe.matmul(out, x[:, k, tb * P:tb * P + P], w[:, r, c:c + 256],
                                            start=(k == 0 and q == 0), stop=(k == KD - 1 and q == 2))
                ins.then_inc(S["unit_done"], 2)
                return
            gl = [g for g in GL if g <= u < g + 12]
            if gl and (u - gl[0]) % 3 == 2:
                s = GL[gl[0]]

                def yk(k):
                    return y_hi[:, s, k, :], y_lo[:, s, k, :]
                for q in range(2):
                    ins = gemm(GB[(o + q) % 4][:, :], u % RING, q * T, yk, range(4))
            elif u == U_SMALL:
                for k in range(KD):
                    for q, (w, x) in enumerate(((w_hi, 0), (w_hi, 1), (w_lo, 0))):
                        ins = pe.matmul(GB[o % 4][0:96, :], w[:, u % RING, 96 * k:96 * k + 96], xn(k)[x],
                                        start=(k == 0 and q == 0), stop=(k == KD - 1 and q == 2))
            else:
                if u == 0:
                    for k in range(KD):
                        pe.wait_ge(S["xn_ready"], k + 1)
                        for q, (w, x) in enumerate(((w_hi, 0), (w_hi, 1), (w_lo, 0))):
                            ins = pe.matmul(GB[0][:, :], w[:, 0, k * P:k * P + P], xn(k)[x],
                                            start=(k == 0 and q == 0), stop=(k == KD - 1 and q == 2))
                else:
                    ins = gemm(GB[o % 4][:, :], u % RING, 0, xn, range(KD))
            ins.then_inc(S["unit_done"], 1)

        pe.wait_ge(S["built"], 14)
        pe.wait_ge(S["n1_sum_in"], KD)
        pe.matmul(X[0][:, :], ones[:], t1[:, 0:T], start=True, stop=True).then_inc(S["n1_sum"], 1)

        for u in range(U_OUT):
            for gfirst, need, cnt in ((U_GL_D, "d_lo", 4), (U_GL_A, "a_lo", 4), (U_GL_B, "b_lo", 4),
                                      (U_GL_C, "c_lo", 4)):
                if u == gfirst + 2:
                    pe.wait_ge(S[need], cnt)
            unit(u)
            if u in D_AT:
                h = D_AT.index(u)
                if h == 0:
                    pe.wait_ge(S["psum_read_dve"], 12 - 4 + 4)
                else:
                    pe.wait_ge(S["d_lo"], h)
                if h == 2:
                    pe.wait_ge(S["g_cols"], 1)
                for j in range(NB):
                    ins = pe.matmul(X[j][:, 0:BLK_W[j]], dk[:, h, j * P:j * P + P], dq[:, h, j * P:T],
                                    start=True, stop=True)
                    ins.then_inc(S["d_scores"], 1)
            if u - 2 in D_AT:
                h = D_AT.index(u - 2)
                pe.wait_ge(S["d_soft"], h + 1)
                for j in range(NB):
                    for jj in range(j, NB):
                        ins = pe.matmul(X[j][:, P * (jj - j):BLK_W[j]], (tri if jj == j else ones)[:],
                                        t1[:, blk(jj)], start=(jj == j), stop=(jj == NB - 1),
                                        skip_group_check=True)
                    ins.then_inc(S["d_suffix"], 1)
            if u - 3 in D_AT:
                h = D_AT.index(u - 3)
                pe.wait_ge(S["d_weights"], h + 1)
                for j in range(NB):
                    ins = pe.matmul(X[0][:, j * P:T], dv[:, j, h * P:h * P + P], t1[:, blk(j)],
                                    start=(j == 0), stop=(j == NB - 1), skip_group_check=True)
                ins.then_inc(S["d_out"], 1)
            if u == 19:
                pe.wait_ge(S["g_rows"], 1)
                pe.wait_ge(S["d_expo"], 2)
                for j in range(NB):
                    ins = pe.transpose(X[3][:, j * P:j * P + P], g_row[:, j * P:j * P + P], ident[:])
                ins.then_inc(S["g_trans"], 1)
            if u in A_AT:
                h = A_AT.index(u)
                p0 = 64 * (h % 2)
                if h == 0:
                    pe.wait_ge(S["d_lo"], 4)
                    pe.wait_ge(S["psum_read_dve"], order[first_tile[U_AO] - 1][1])
                else:
                    pe.wait_ge(S["a_rstd"], h)
                for j in range(NB):
                    ins = pe.matmul(X[j][:, 0:BLK_W[j]], ak[p0:p0 + 64, h // 2, j * P:j * P + P],
                                    aq[p0:p0 + 64, h // 2, j * P:T], start=True, stop=True)
                    ins.then_inc(S["a_scores"], 1)
            if u - 2 in A_AT:
                h = A_AT.index(u - 2)
                pe.wait_ge(S["a_w"], h + 1)
                for b, w in ((0, None), (1, ones)):
                    for j in range(NB):
                        lhs = ones[:] if b else av[:, j, h * P:h * P + P]
                        ins = pe.matmul(X[b][:, j * P:T], lhs, t0[:, blk(j)], start=(j == 0),
                                        stop=(j == NB - 1), skip_group_check=True)
                ins.then_inc(S["a_numden"], 1)
            if u - 4 in A_AT:
                h = A_AT.index(u - 4)
                pe.wait_ge(S["a_sq"], h + 1)
                pe.matmul(X[2][:, :], ones[:], t1[:, T:2 * T], start=True, stop=True).then_inc(S["a_sum"], 1)
            if u == 51:
                pe.wait_ge(S["z_made"], 8)
                pe.wait_ge(S["a_rstd"], 4)
                for b in range(NB):
                    for c in range(4):
                        ins = pe.transpose(X[b][:, c * P:c * P + P], xbc[:, c, b * P:b * P + P], ident[:])
                    ins.then_inc(S["c_trans"], 1)
            if u in (52, 61):
                g = 0 if u == 52 else 1
                if g == 0:
                    pe.wait_ge(S["c_xdt"], 4)
                else:
                    pe.wait_ge(S["c_z"], 2)
                for j in range(NB):
                    ins = pe.matmul(X[j][:, 0:BLK_W[j]], xbc[:, 4 + g, j * P:j * P + P], xbc[:, 6 + g, j * P:T],
                                    start=True, stop=True)
                    ins.then_inc(S["c_cb"], 1)
            if u - 1 in C_AT:
                h = C_AT.index(u - 1)
                pe.wait_ge(S["c_w"], h + 1)
                if h % 2 == 0 and h // 2 >= 2:
                    pe.wait_ge(S["c_z"], h // 2 - 1)
                if h in (0, 4):
                    pe.wait_ge(S["c_cbm"], 4 * (h // 4 + 1))
                tt = (t0, t1)[h % 2]
                for j in range(NB):
                    ins = pe.matmul(X[(h // 2) % 2][64 * (h % 2):64 * (h % 2) + 64, j * P:T],
                                    xdt[:, j, h * 64:h * 64 + 64], tt[:, blk(j)],
                                    start=(j == 0), stop=(j == NB - 1), skip_group_check=True)
                ins.then_inc(S["c_y"], 1)
            if u == 71:
                pe.wait_ge(S["c_acc"], 1)
                pe.matmul(X[2][:, :], ones[:], t0[:, 0:T], start=True, stop=True).then_inc(S["c_sum"], 1)

        def mg(k):
            return (y_hi[:, 0, k, :], y_lo[:, 0, k, :]) if k < 4 else (xn_hi[:, k, :], xn_lo[:, k, :])
        pe.wait_ge(S["psum_read_act"], ACT0)
        pe.wait_ge(S["merged_ready"], KD)
        with pe.Fori(0, KD // 4) as i:
            for q in range(4):
                pe.wait_ge(S["lo_ready"], U_OUT + 4 * i + q + 1)
                pe.wait_ge(S["psum_read_dve"], DVE0 - 3 + 4 * i + q)
                gemm(GB[(TILES0 + q) % 4][:, :], (U_OUT + q) % RING, 0, mg, range(KD)).then_inc(S["unit_done"], 1)
        pe.wait_ge(S["wo_acc"], KD)
        pe.matmul(X[0][:, :], ones[:], f_ac[:], start=True, stop=True).then_inc(S["n2_sum"], 1)
        pe.wait_ge(S["n2_ready"], KD)
        with pe.Fori(0, 2 * NFF // 4) as i:
            for q in range(4):
                pe.wait_ge(S["lo_ready"], U_UP + 4 * i + q + 1)
                pe.wait_ge(S["psum_read_dve"], DVE0 + KD - 3 + 4 * i + q)
                gemm(GB[(TILES0 + q) % 4][:, :], (U_UP + q) % RING, 0, xn, range(KD)).then_inc(S["unit_done"], 1)
        pe.wait_ge(S["f_lo"], NFF)
        def hk(k):
            return h_hi[:, k, :], h_lo[:, k, :]
        with pe.Fori(0, KD // 2) as i:
            for t in range(2):
                for q in range(4):
                    pe.wait_ge(S["lo_ready"], U_DOWN + 8 * i + 4 * t + q + 1)
                    if q == 0:
                        pe.wait_ge(S["psum_read_dve"], DVE0 + KD + 2 * NFF - 1 + 2 * i + t)
                    gemm(GB[t][:, :], (U_DOWN + q) % RING, 0, hk, range(DOWN_K0[q], DOWN_K0[q] + DOWN_K[q]),
                         first=(q == 0), last_=(q == 3)).then_inc(S["unit_done"], 1)
        pe.wait_ge(S["o_acc"], KD)
        pe.matmul(X[0][:, :], ones[:], f_ac[:], start=True, stop=True).then_inc(S["o_sum"], 1)

    @block.scalar
    def _(act):
        own = [0]

        def link(ins):
            own[0] = own[0] + 1
            ins.then_inc(S["act_own"], 1)
            act.wait_ge(S["act_own"], own[0])

        def hi(u, r, rep, n=1024):
            act.wait_ge(S[f"raw{r}"], 16 * rep + 16)
            act.activation(w_hi[:, r, 0:n], raw[:, r, 0:n], ACT.Copy).then_inc(S["hi_ready"], 1)

        def rstd(out, summed, n):
            link(act.activation(out, summed, ACT.Ln, bias=cst[:, 1:2], scale=1.0 / n))
            return act.activation(out, out, ACT.Exp, scale=-0.5)

        act.wait_ge(S["built"], 14)
        act.wait_ge(S["vec_loaded"], 32)
        for k in range(KD):
            act.wait_ge(S["x_loaded"], 16 * KD)
            if k >= 2:
                act.wait_ge(S["n1_sum_in"], k - 1)
            act.activation(t0[:, (k % 2) * T:(k % 2) * T + T], x_in[:, k, :], ACT.Square).then_inc(S["n1_sqr"], 1)
        for r in range(RING):
            hi(r, r, 0)
        act.wait_ge(S["n1_sum"], 1)
        rstd(t0[:, 0:T], X[0][:, :], D).then_inc(S["n1_rstd"], 1)
        for k in range(KD):
            act.wait_ge(S["n1_xn"], k + 1)
            act.activation(xn_hi[:, k, :], x_in[:, k, :], ACT.Copy).then_inc(S["n1_hi"], 1)

        def evac(u):
            if made[u][0] == 0:
                return
            o = first_tile[u]
            ps = GB[o % 4]
            if U_AO <= u < U_AO + 4:
                act.activation(ao[:, u - U_AO, :], ps[:, :], ACT.Sigmoid).then_inc(S["psum_read_act"], 1)
            elif U_Z <= u < U_Z + 4:
                act.activation(zy[:, u - U_Z, :], ps[:, :], ACT.Silu).then_inc(S["psum_read_act"], 1)
            elif U_XBC <= u < U_XBC + 8:
                c = u - U_XBC
                if c >= 2:
                    act.wait_ge(S["z_made"], c - 1)
                act.activation(stg[:, c % 2, :], ps[:, :], ACT.Identity, bias=vec[:, V_CCB + c:V_CCB + c + 1],
                               scale=vec[:, V_CCW + 4 * c + 3:V_CCW + 4 * c + 4]).then_inc(S["x_tap"], 1)
                act.wait_ge(S["psum_read_dve"], order[o][1])
                act.activation(xbc[:, c, :], stg[:, c % 2, :], ACT.Silu).then_inc(S["z_made"], 1)
            for g in GL:
                if g <= u < g + 12 and (u - g) % 3 < 2:
                    n = list(GL).index(g) * 4 + (u - g) // 3
                    if n == 0:
                        act.wait_ge(S["d_lo"], 4)
                    if 2 <= n < 6:
                        act.wait_ge(S["psum_read_dve"], order[first_tile[U_GL_D + 3 * (n - 2) + 2] + 1][1])
                    elif n >= 6:
                        act.wait_ge(S["merged_put"], 2 * (n - 5))
                    act.activation(gate[:, n % 2, (u - g) % 3, :], ps[:, :], ACT.Sigmoid)\
                        .then_inc(S["psum_read_act"], 1)

        for u in range(U_OUT):
            act.wait_ge(S["unit_done"], u + 1)
            hi(u + RING, u % RING, (u + RING) // RING)
            evac(u)
            s = u + 1
            if s - 1 in D_AT:
                h = D_AT.index(s - 1)
                act.wait_ge(S["d_masked"], h + 1)
                if h:
                    act.wait_ge(S["d_out"], h)
                link(act.activation(t1[:], t0[:], ACT.Abs))
                link(act.activation(t1[:], t1[:], ACT.Exp, scale=-1.0))
                act.activation(t1[:], t1[:], ACT.Ln, bias=cst[:, 0:1]).then_inc(S["d_soft_in"], 1)
            if s - 3 in D_AT:
                h = D_AT.index(s - 3)
                act.wait_ge(S["d_expo"], h + 1)
                act.activation(t1[:], t0[:], ACT.Exp).then_inc(S["d_weights"], 1)
            if s - 4 in D_AT:
                h = D_AT.index(s - 4)
                act.wait_ge(S["d_out"], h + 1)
                act.activation(y_hi[:, 0, h, :], X[0][:, :], ACT.Copy).then_inc(S["d_hi"], 1)
            if s == 14:
                act.wait_ge(S["psum_read_dve"], order[first_tile[U_SMALL]][1])
                link(act.activation(g_ab[:], g_x[:], ACT.Abs))
                link(act.activation(g_ab[:], g_ab[:], ACT.Exp, scale=-1.0))
                act.activation(g_ab[:], g_ab[:], ACT.Ln, bias=cst[0:40, 0:1]).then_inc(S["g_log"], 1)
                act.activation(rsm[32:40, 3:4], rsm[32:40, 2:3], ACT.Exp).then_inc(S["g_log"], 1)
            if s == 18:
                act.wait_ge(S["g_rows"], 1)
                act.activation(g_nm[:, 1, :], g_nm[:, 1, :], ACT.Exp).then_inc(S["g_en"], 1)
            if s in A_AT:
                h = A_AT.index(s)
                act.wait_ge(S["a_arg"], 4 * (h + 1))
                act.activation(t0[:], t0[:], ACT.Exp).then_inc(S["a_dec"], 1)
            if s - 4 in A_AT:
                h = A_AT.index(s - 4)
                act.wait_ge(S["a_h"], h + 1)
                act.activation(t1[:, T:2 * T], t1[:, 0:T], ACT.Square).then_inc(S["a_sq"], 1)
            if s - 5 in A_AT:
                h = A_AT.index(s - 5)
                act.wait_ge(S["a_sum"], h + 1)
                link(act.activation(t1[:, T:2 * T], X[2][:, :], ACT.Ln,
                                    bias=cst[:, 1:2], scale=1.0 / P))
                act.activation(t1[:, T:2 * T], t1[:, T:2 * T], ACT.Exp, scale=-0.5).then_inc(S["a_rstd"], 1)
            if s - 6 in A_AT:
                h = A_AT.index(s - 6)
                act.wait_ge(S["a_y"], 2 * h + 2)
                act.activation(y_hi[:, 1, h, :], t1[:, 0:T], ACT.Copy).then_inc(S["a_hi"], 1)
            if U_B <= s - 1 < U_B + 12 and (s - 1 - U_B) % 3 == 2:
                c = (s - 1 - U_B) // 3
                act.wait_ge(S["psum_read_dve"], order[first_tile[U_B + 3 * c + 2]][1])
                if c == 0:
                    act.wait_ge(S["unit_done"], U_GL_D + 12)
                act.activation(y_hi[:, 0, c, :], stg[:, 1, :], ACT.Copy).then_inc(S["b_hi"], 1)
            if s in C_AT:
                h = C_AT.index(s)
                tt = (t0, t1)[h % 2]
                act.wait_ge(S["c_arg"], 4 * (h + 1))
                act.activation(tt[:], tt[:], ACT.Exp).then_inc(S["c_dec"], 1)
            if s == 70:
                act.wait_ge(S["c_y"], C_HEADS)
                act.wait_ge(S["c_fin"], 4)
                for c in range(4):
                    tt = (t0, t1)[c // 2]
                    act.activation(tt[:, (c % 2) * T:(c % 2) * T + T], zy[:, c, :], ACT.Square)\
                        .then_inc(S["c_sq"], 1)
            if s == 72:
                act.wait_ge(S["c_sum"], 1)
                rstd(t1[:, 0:T], X[2][:, :], T).then_inc(S["c_rstd"], 1)
            if s == 75:
                act.wait_ge(S["unit_done"], U_GL_A + 12)
                for c in range(4):
                    act.wait_ge(S["c_fin"], 5 + c)
                    act.activation(y_hi[:, 1, c, :], zy[:, c, :], ACT.Copy).then_inc(S["c_hi"], 1)
            for p in range(2):
                if s == U_GL_C + 3 * p + 4:
                    for k in (2 * p, 2 * p + 1):
                        act.wait_ge(S["merged_put"], 2 * KD + k + 1)
                        act.activation(y_hi[:, 0, k, :], merged[:, k, :], ACT.Copy).then_inc(S["merged_hi"], 1)
        for k in range(4, KD):
            act.wait_ge(S["merged_put"], 2 * KD + k + 1)
            act.activation(xn_hi[:, k, :], merged[:, k, :], ACT.Copy).then_inc(S["merged_hi"], 1)

        def hi_loop(u, r, i, n=1024):
            act.wait_ge(S["unit_done"], u + 1)
            hi(0, r, i, n)

        act.wait_ge(S["c_lo"], 4)
        with act.Fori(0, KD // 4) as i:
            for q in range(4):
                hi_loop(U_OUT + 4 * i + q, (U_OUT + q) % RING, (U_OUT + q + RING) // RING + i)
                act.wait_ge(S["psum_read_dve"], DVE0 + 4 * i + q + 1)
                act.activation(f_sq[:], x1[:, 4 * i + q, :], ACT.Square).then_inc(S["wo_sq"], 1)
                act.wait_ge(S["wo_acc"], 4 * i + q + 1)
        act.wait_ge(S["n2_sum"], 1)
        rstd(f_rs[:], X[0][:, :], D).then_inc(S["n2_rstd"], 1)
        for k in range(KD):
            act.wait_ge(S["n2_xn"], k + 1)
            act.activation(xn_hi[:, k, :], f_cv[:, 0, k % 2, :], ACT.Copy).then_inc(S["n2_hi"], 1)

        with act.Fori(0, 2 * NFF // 4) as i:
            for q in range(4):
                side, half = q % 2, q // 2
                hi_loop(U_UP + 4 * i + q, (U_UP + q) % RING, (U_UP + q + RING) // RING + i)
                act.activation(f_cv[:, half, side, :], GB[(TILES0 + q) % 4][:, :], ACT.Identity,
                               bias=fcw[:, 4 * i + q, 3:4],
                               scale=fcw[:, 4 * i + q, 2:3]).then_inc(S["f_tap"], 1)
                if side == 1:
                    act.wait_ge(S["psum_read_dve"], DVE0 + KD + 4 * i + q)
                    act.activation(f_si[:], f_cv[:, half, 0, :], ACT.Silu).then_inc(S["f_silu"], 1)
                    act.wait_ge(S["f_h"], 2 * i + half + 1)
                    act.activation(h_hi[:, 2 * i + half, :], f_cv[:, half, 1, :], ACT.Copy).then_inc(S["f_hi"], 1)
        def down(i, t, more=True):
            for q in range(4):
                if more or t == 0:
                    hi_loop(U_DOWN + 8 * i + 4 * t + q, (U_DOWN + q) % RING,
                            (U_DOWN + q + RING) // RING + 2 * i + t, DOWN_K[q] * P)
            act.wait_ge(S["psum_read_dve"], DVE0 + KD + 2 * NFF + 2 * i + t + 1)
            act.activation(f_sq[:], x1[:, 2 * i + t, :], ACT.Square).then_inc(S["o_sq"], 1)
            act.wait_ge(S["o_acc"], 2 * i + t + 1)
        with act.Fori(0, KD // 2 - 1) as i:
            for t in range(2):
                down(i, t)
        for t in range(2):
            down(KD // 2 - 1, t, more=False)
        act.wait_ge(S["o_sum"], 1)
        rstd(f_rs[:], X[0][:, :], D).then_inc(S["o_rstd"], 1)

    @block.vector
    def _(dve):
        own = [0]

        def link(ins):
            own[0] = own[0] + 1
            ins.then_inc(S["dve_own"], 1)
            dve.wait_ge(S["dve_own"], own[0])

        def lo(u, r, n=1024):
            dve.wait_ge(S["hi_ready"], u + 1)
            dve.tensor_tensor(w_lo[:, r, 0:n], raw[:, r, 0:n], w_hi[:, r, 0:n].bitcast(F32), ALU.subtract)\
                .then_inc(S["lo_ready"], 1)

        def split_lo(out, x, high):
            return dve.tensor_tensor(out, x, high.bitcast(F32), ALU.subtract)

        dve.wait_ge(S["built"], 14)
        dve.wait_ge(S["vec_loaded"], 32)
        for k in range(KD):
            dve.wait_ge(S["n1_sqr"], k + 1)
            sq = t0[:, (k % 2) * T:(k % 2) * T + T]
            if k == 0:
                ins = dve.tensor_copy(t1[:, 0:T], sq)
            else:
                ins = dve.tensor_tensor(t1[:, 0:T], t1[:, 0:T], sq, ALU.add)
            ins.then_inc(S["n1_sum_in"], 1)
            dve.wait_ge(S["n1_sum_in"], k + 1)
        for r in range(RING):
            lo(r, r)
        dve.wait_ge(S["n1_rstd"], 1)
        for k in range(KD):
            dve.scalar_tensor_tensor(out=x_in[:, k, :], in0=x_in[:, k, :], scalar=vec[:, V_MIX + k:V_MIX + k + 1],
                                     in1=t0[:, 0:T], op0=ALU.mult, op1=ALU.mult).then_inc(S["n1_xn"], 1)
            dve.wait_ge(S["n1_hi"], k + 1)
            split_lo(xn_lo[:, k, :], x_in[:, k, :], xn_hi[:, k, :]).then_inc(S["xn_ready"], 1)

        def evac(u):
            n = made[u][0]
            if n == 0:
                return
            o = first_tile[u]
            ps = GB[o % 4]

            def read(ins):
                ins.then_inc(S["psum_read_dve"], 1)
            if u < U_DK:
                if u == 0:
                    dve.wait_ge(S["xn_ready"], KD)
                read(dve.tensor_scalar(dq[:, u, :], ps[:, :], D_SCALE, None, ALU.mult))
            elif u < U_DV:
                read(dve.tensor_copy(dk[:, u - U_DK, :], ps[:, :]))
            elif u < U_DV + 4 or U_AV <= u < U_AV + 4:
                dst, c = (dv, (u - U_DV) // 2) if u < U_DV + 4 else (av, (u - U_AV) // 2)
                for q in range(2):
                    read(dve.tensor_copy(dst[:, 2 * q:2 * q + 2, 256 * c:256 * c + 256],
                                         GB[(o + q) % 4][:, :].rearrange("p (b c) -> p b c", b=2)))
            elif u == U_SMALL:
                link(dve.tensor_scalar(g_i[:], ps[0:4, :], rsm[0:4, 0:1], None, ALU.add))
                link(dve.tensor_scalar(g_x[0:4, :], ps[32:36, :], rsm[0:4, 1:2], -1.0, ALU.add, ALU.mult))
                dve.tensor_scalar(g_x[32:40, :], ps[64:72, :], rsm[32:40, 1:2], None, ALU.add)\
                    .then_inc(S["psum_read_dve"], 1)
            elif U_AQ <= u < U_AK:
                read(dve.tensor_scalar(aq[:, u - U_AQ, :], ps[:, :], A_SCALE, None, ALU.mult))
            elif U_AK <= u < U_AV:
                read(dve.tensor_copy(ak[:, u - U_AK, :], ps[:, :]))
            elif U_XBC <= u < U_XBC + 8:
                c = u - U_XBC
                w = stg[:, c % 2, :]
                dve.wait_ge(S["x_tap"], c + 1)
                for back in (1, 2, 3):
                    tap = V_CCW + 4 * c + 3 - back
                    ins = dve.scalar_tensor_tensor(out=w[:, back:T], in0=ps[:, 0:T - back],
                                                   scalar=vec[:, tap:tap + 1], in1=w[:, back:T],
                                                   op0=ALU.mult, op1=ALU.add)
                    if back < 3:
                        link(ins)
                read(ins)
            elif U_B <= u < U_B + 12:
                c, what = (u - U_B) // 3, (u - U_B) % 3
                if what == 0:
                    if c == 0:
                        dve.wait_ge(S["z_made"], 8)
                    read(dve.tensor_copy(stg[:, 0, :], ps[:, :]))
                elif what == 1:
                    dve.wait_ge(S["psum_read_dve"], order[o - 1][1])
                    ins = dve.tensor_tensor(stg[:, 0, :], ps[:, :], stg[:, 0, :], ALU.mult)
                    read(ins)
                    dve.wait_ge(S["psum_read_dve"], order[o][1])
                    if c:
                        dve.wait_ge(S["b_hi"], c)
                    tap = V_BCW + 3 * c
                    link(dve.tensor_scalar(stg[:, 1, :], stg[:, 0, :], vec[:, tap + 2:tap + 3], None, ALU.mult))
                    for back in (1, 2):
                        link(dve.scalar_tensor_tensor(out=stg[:, 1, back:T], in0=stg[:, 0, 0:T - back],
                                                      scalar=vec[:, tap + 2 - back:tap + 3 - back],
                                                      in1=stg[:, 1, back:T], op0=ALU.mult, op1=ALU.add))
                else:
                    read(dve.tensor_tensor(stg[:, 1, :], ps[:, :], stg[:, 1, :], ALU.mult))
            for g in GL:
                if g <= u < g + 12 and (u - g) % 3 == 2:
                    b = list(GL).index(g)
                    t = (u - g) // 3
                    n = 4 * b + t
                    for q in range(2):
                        k = 2 * t + q
                        dve.wait_ge(S["psum_read_act"], order[o - 2 + q][1])
                        gt = gate[:, n % 2, q, :]
                        ps = GB[(o + q) % 4]
                        if b == 0:
                            dve.tensor_tensor(merged[:, k, :], ps[:, :], gt, ALU.mult)\
                                .then_inc(S["psum_read_dve"], 1)
                        else:
                            dve.tensor_tensor(gt, ps[:, :], gt, ALU.mult).then_inc(S["psum_read_dve"], 1)
                            dve.wait_ge(S["psum_read_dve"], order[o + q][1])
                            if b >= 2:
                                dve.wait_ge(S["merged_put"], KD * (b - 2) + k + 1)
                            dve.tensor_tensor(merged[:, k, :], merged[:, k, :], gt, ALU.add)\
                                .then_inc(S["merged_put"], 1)

        for u in range(U_OUT):
            lo(u + RING, u % RING)
            evac(u)
            s = u + 1
            if s - 1 in D_AT:
                h = D_AT.index(s - 1)
                if h:
                    dve.wait_ge(S["d_weights"], h)
                for j in range(NB):
                    dve.wait_ge(S["d_scores"], NB * h + j + 1)
                    ins = dve.tensor_tensor(t0[:, blk(j)], X[j][:, 0:BLK_W[j]], negm[:, 0:BLK_W[j]], ALU.add)
                ins.then_inc(S["d_masked"], 1)
            if s - 2 in D_AT:
                h = D_AT.index(s - 2)
                dve.wait_ge(S["d_soft_in"], h + 1)
                dve.scalar_tensor_tensor(out=t1[:], in0=t0[:], scalar=0.0, in1=t1[:], op0=ALU.max,
                                         op1=ALU.add).then_inc(S["d_soft"], 1)
            if s - 3 in D_AT:
                h = D_AT.index(s - 3)
                for j in range(NB):
                    dve.wait_ge(S["d_suffix"], NB * h + j + 1)
                    ins = dve.tensor_tensor(t0[:, blk(j)], t0[:, blk(j)], X[j][:, 0:BLK_W[j]], ALU.subtract)
                ins.then_inc(S["d_expo"], 1)
            if s - 4 in D_AT:
                h = D_AT.index(s - 4)
                dve.wait_ge(S["d_hi"], h + 1)
                split_lo(y_lo[:, 0, h, :], X[0][:, :], y_hi[:, 0, h, :]).then_inc(S["d_lo"], 1)
            if s == 15:
                dve.wait_ge(S["g_log"], 2)
                link(dve.scalar_tensor_tensor(out=g_sp[:], in0=g_x[:], scalar=0.0, in1=g_ab[:], op0=ALU.max,
                                              op1=ALU.add))
                link(dve.tensor_tensor_scan(g_b[0:4, :], g_one[0:4, :], g_sp[0:4, :], 0.0, ALU.mult, ALU.add))
                link(dve.tensor_tensor(g_row[0:4, :], g_i[:], g_b[0:4, :], ALU.add))
                link(dve.tensor_tensor_scan(g_i[:], g_row[0:4, :], g_row[0:4, :], 0.0, ALU.max, ALU.max))
                link(dve.tensor_scalar(g_b[32:40, :], g_sp[32:40, :], rsm[32:40, 3:4], -1.0, ALU.mult, ALU.mult))
            if s == 16:
                link(dve.tensor_scalar(g_nm[:, 0, :], g_i[:], -1.0, None, ALU.mult))
                link(dve.tensor_tensor(g_nm[:, 1, :], g_b[0:4, :], g_i[:], ALU.subtract))
                link(dve.tensor_copy(g_row[32:40, :], g_sp[32:40, :]))
            if s == 17:
                for j in range(NB):
                    link(dve.tensor_tensor_scan(a_run[32:40, blk(j)], g_one[32:40, 0:BLK_W[j]],
                                                g_b[32:40, j * P:T], 0.0, ALU.mult, ALU.add))
                for j in range(NB):
                    ins = dve.tensor_copy(g_row[64:72, j * P:j * P + P], a_run[32:40, diag(j)])
                    if j < NB - 1:
                        link(ins)
                ins.then_inc(S["g_rows"], 1)
            if s == 20:
                dve.wait_ge(S["g_trans"], 1)
                dve.tensor_copy(colT[:, :, :], X[3][:, :].rearrange("p (b c) -> p b c", b=NB))\
                    .then_inc(S["g_cols"], 1)
                dve.wait_ge(S["g_cols"], 1)
            if s in A_AT:
                h = A_AT.index(s)
                dve.wait_ge(S["a_nm"], 16 * (h + 1))
                if h:
                    dve.wait_ge(S["a_numden"], h)
                else:
                    dve.wait_ge(S["d_weights"], 4)
                for j in range(NB):
                    dve.tensor_scalar(t0[:, blk(j)], nmb[:, j * P:T], colT[:, j, h:h + 1], 0.0, ALU.add,
                                      ALU.min).then_inc(S["a_arg"], 1)
            if s - 1 in A_AT:
                h = A_AT.index(s - 1)
                dve.wait_ge(S["a_dec"], h + 1)
                for j in range(NB):
                    dve.wait_ge(S["a_scores"], NB * h + j + 1)
                    ins = dve.tensor_tensor(t0[:, blk(j)], t0[:, blk(j)], X[j][:, 0:BLK_W[j]], ALU.mult)
                link(ins)
                for j in range(NB):
                    ins = dve.tensor_tensor(t0[:, diag(j)], t0[:, diag(j)], causal[:], ALU.mult)
                ins.then_inc(S["a_w"], 1)
            if s - 3 in A_AT:
                h = A_AT.index(s - 3)
                dve.wait_ge(S["a_numden"], h + 1)
                dve.wait_ge(S["a_en"], 16 * (h + 1))
                if h:
                    dve.wait_ge(S["a_lo"], h)
                else:
                    dve.wait_ge(S["d_out"], 4)
                link(dve.scalar_tensor_tensor(out=t1[:, T:2 * T], in0=X[1][:, :], scalar=-1.0, in1=enb[:],
                                              op0=ALU.mult, op1=ALU.max))
                link(dve.tensor_tensor(t1[:, T:2 * T], X[1][:, :], t1[:, T:2 * T], ALU.max))
                link(dve.reciprocal(t1[:, T:2 * T], t1[:, T:2 * T]))
                dve.tensor_tensor(t1[:, 0:T], X[0][:, :], t1[:, T:2 * T], ALU.mult).then_inc(S["a_h"], 1)
            if s - 5 in A_AT:
                h = A_AT.index(s - 5)
                dve.wait_ge(S["a_rstd"], h + 1)
                dve.wait_ge(S["psum_read_act"], order[first_tile[U_AO + 3]][1])
                dve.scalar_tensor_tensor(out=t1[:, 0:T], in0=t1[:, 0:T], scalar=vec[:, V_AG + h:V_AG + h + 1],
                                         in1=t1[:, T:2 * T], op0=ALU.mult, op1=ALU.mult).then_inc(S["a_y"], 1)
                dve.wait_ge(S["a_y"], 2 * h + 1)
                dve.tensor_tensor(t1[:, 0:T], t1[:, 0:T], ao[:, h, :], ALU.mult).then_inc(S["a_y"], 1)
            if s - 6 in A_AT:
                h = A_AT.index(s - 6)
                dve.wait_ge(S["a_hi"], h + 1)
                split_lo(y_lo[:, 1, h, :], t1[:, 0:T], y_hi[:, 1, h, :]).then_inc(S["a_lo"], 1)
            if U_B <= s - 1 < U_B + 12 and (s - 1 - U_B) % 3 == 2:
                c = (s - 1 - U_B) // 3
                dve.wait_ge(S["b_hi"], c + 1)
                split_lo(y_lo[:, 0, c, :], stg[:, 1, :], y_hi[:, 0, c, :]).then_inc(S["b_lo"], 1)
            if s == 52:
                dve.wait_ge(S["a_lo"], 4)
                for b in range(NB):
                    dve.wait_ge(S["c_trans"], b + 1)
                    dve.tensor_tensor(xdt[:, b, :].rearrange("p (h c) -> p h c", h=C_HEADS),
                                      X[b][:, :].rearrange("p (h c) -> p h c", h=C_HEADS),
                                      colT[:, b, 32:40].unsqueeze(2).to_broadcast([P, C_HEADS, 64]),
                                      ALU.mult).then_inc(S["c_xdt"], 1)
            if s in (53, 62):
                g = 0 if s == 53 else 1
                for j in range(NB):
                    dve.wait_ge(S["c_cb"], NB * g + j + 1)
                    dve.tensor_tensor(cbm[:, diag(j)], X[j][:, 0:P], causal[:], ALU.mult).then_inc(S["c_cbm"], 1)
                    if j < NB - 1:
                        dve.tensor_copy(cbm[:, BLK_O[j] + P:BLK_O[j] + BLK_W[j]], X[j][:, P:BLK_W[j]])\
                            .then_inc(S["dve_own"], 1)
                        own[0] += 1
            if s in C_AT:
                h = C_AT.index(s)
                tt = (t0, t1)[h % 2]
                dve.wait_ge(S["c_abc"], 16 * (h + 1))
                if h >= 2:
                    dve.wait_ge(S["c_y"], h - 1)
                for j in range(NB):
                    dve.tensor_scalar(tt[:, blk(j)], abc[:, blk(j)], colT[:, j, 64 + h:65 + h], 0.0,
                                      ALU.subtract, ALU.min).then_inc(S["c_arg"], 1)
            if s - 1 in C_AT:
                h = C_AT.index(s - 1)
                tt = (t0, t1)[h % 2]
                dve.wait_ge(S["c_dec"], h + 1)
                dve.wait_ge(S["dve_own"], own[0])
                dve.wait_ge(S["c_cbm"], NB * (h // 4 + 1))
                dve.tensor_tensor(tt[:], tt[:], cbm[:], ALU.mult).then_inc(S["c_w"], 1)
            if s in (57, 61, 65, 69):
                p = (s - 57) // 4
                dve.wait_ge(S["c_y"], 2 * p + 2)
                xs = xbc[:, p, :]
                if p == 0:
                    dve.wait_ge(S["z_made"], 8)
                    dve.wait_ge(S["psum_read_act"], order[first_tile[U_Z + 3]][1])
                dve.scalar_tensor_tensor(out=xs, in0=xs, scalar=vec[:, V_DSK + p:V_DSK + p + 1],
                                         in1=X[p % 2][:, :], op0=ALU.mult, op1=ALU.add).then_inc(S["c_z"], 1)
                dve.wait_ge(S["c_z"], p + 1)
                dve.tensor_tensor(zy[:, p, :], zy[:, p, :], xs, ALU.mult).then_inc(S["c_fin"], 1)
            if s == 71:
                dve.wait_ge(S["c_sq"], 4)
                link(dve.tensor_tensor(t0[:, 0:T], t0[:, 0:T], t0[:, T:2 * T], ALU.add))
                link(dve.tensor_tensor(t0[:, 0:T], t0[:, 0:T], t1[:, 0:T], ALU.add))
                dve.tensor_tensor(t0[:, 0:T], t0[:, 0:T], t1[:, T:2 * T], ALU.add).then_inc(S["c_acc"], 1)
            if s == 74:
                dve.wait_ge(S["c_rstd"], 1)
                dve.wait_ge(S["c_fin"], 4)
                for c in range(4):
                    dve.scalar_tensor_tensor(out=zy[:, c, :], in0=zy[:, c, :],
                                             scalar=vec[:, V_CNG + c:V_CNG + c + 1], in1=t1[:, 0:T],
                                             op0=ALU.mult, op1=ALU.mult).then_inc(S["c_fin"], 1)
            if s == 76:
                for c in range(4):
                    dve.wait_ge(S["c_hi"], c + 1)
                    split_lo(y_lo[:, 1, c, :], zy[:, c, :], y_hi[:, 1, c, :]).then_inc(S["c_lo"], 1)
            for p in range(2):
                if s == U_GL_C + 3 * p + 4:
                    for k in (2 * p, 2 * p + 1):
                        dve.wait_ge(S["merged_hi"], k + 1)
                        split_lo(y_lo[:, 0, k, :], merged[:, k, :], y_hi[:, 0, k, :])\
                            .then_inc(S["merged_ready"], 1)
        for k in range(4, KD):
            dve.wait_ge(S["merged_hi"], k + 1)
            split_lo(xn_lo[:, k, :], merged[:, k, :], xn_hi[:, k, :]).then_inc(S["merged_ready"], 1)

        dve.wait_ge(S["x_again"], 16)
        dve.memset(f_ac[:], 0.0).then_inc(S["dve_own"], 1)
        own[0] += 1
        dve.wait_ge(S["dve_own"], own[0])
        with dve.Fori(0, KD // 4) as i:
            for q in range(4):
                r = (U_OUT + q) % RING
                lo(U_OUT + RING + 4 * i + q, r)
                k = 4 * i + q
                dve.tensor_tensor(x1[:, k, :], GB[(TILES0 + q) % 4][:, :], x1[:, k, :], ALU.add)\
                    .then_inc(S["psum_read_dve"], 1)
                dve.wait_ge(S["wo_sq"], k + 1)
                dve.tensor_tensor(f_ac[:], f_ac[:], f_sq[:], ALU.add).then_inc(S["wo_acc"], 1)
                dve.wait_ge(S["wo_acc"], k + 1)
        dve.wait_ge(S["n2_rstd"], 1)
        for k in range(KD):
            if k >= 2:
                dve.wait_ge(S["n2_ready"], k - 1)
            cv = f_cv[:, 0, k % 2, :]
            dve.scalar_tensor_tensor(out=cv, in0=x1[:, k, :], scalar=vec[:, V_FFN + k:V_FFN + k + 1],
                                     in1=f_rs[:], op0=ALU.mult, op1=ALU.mult).then_inc(S["n2_xn"], 1)
            dve.wait_ge(S["n2_hi"], k + 1)
            split_lo(xn_lo[:, k, :], cv, xn_hi[:, k, :]).then_inc(S["n2_ready"], 1)

        with dve.Fori(0, 2 * NFF // 4) as i:
            for q in range(4):
                side, half = q % 2, q // 2
                lo(U_UP + RING + 4 * i + q, (U_UP + q) % RING)
                dve.wait_ge(S["f_tap"], 4 * i + q + 1)
                w, ps = f_cv[:, half, side, :], GB[(TILES0 + q) % 4]
                dve.scalar_tensor_tensor(out=w[:, 1:T], in0=ps[:, 0:T - 1], scalar=fcw[:, 4 * i + q, 1:2],
                                         in1=w[:, 1:T], op0=ALU.mult, op1=ALU.add).then_inc(S["f_tap1"], 1)
                dve.wait_ge(S["f_tap1"], 4 * i + q + 1)
                dve.scalar_tensor_tensor(out=w[:, 2:T], in0=ps[:, 0:T - 2], scalar=fcw[:, 4 * i + q, 0:1],
                                         in1=w[:, 2:T], op0=ALU.mult, op1=ALU.add)\
                    .then_inc(S["psum_read_dve"], 1)
                if side == 1:
                    dve.wait_ge(S["psum_read_dve"], DVE0 + KD + 4 * i + q + 1)
                    dve.wait_ge(S["f_silu"], 2 * i + half + 1)
                    dve.tensor_tensor(w, w, f_si[:], ALU.mult).then_inc(S["f_h"], 1)
                    dve.wait_ge(S["f_hi"], 2 * i + half + 1)
                    split_lo(h_lo[:, 2 * i + half, :], w, h_hi[:, 2 * i + half, :]).then_inc(S["f_lo"], 1)

        dve.memset(f_ac[:], 0.0).then_inc(S["dve_own"], 1)
        own[0] += 1
        dve.wait_ge(S["dve_own"], own[0])

        def down(i, t, more=True):
            k = 2 * i + t
            for q in range(4):
                if more or t == 0:
                    lo(U_DOWN + RING + 4 * k + q, (U_DOWN + q) % RING, DOWN_K[q] * P)
            dve.wait_ge(S["unit_done"], U_DOWN + 4 * k + 4)
            dve.tensor_tensor(x1[:, k, :], GB[t][:, :], x1[:, k, :], ALU.add)\
                .then_inc(S["psum_read_dve"], 1)
            dve.wait_ge(S["o_sq"], k + 1)
            dve.tensor_tensor(f_ac[:], f_ac[:], f_sq[:], ALU.add).then_inc(S["o_acc"], 1)
            dve.wait_ge(S["o_acc"], k + 1)
        with dve.Fori(0, KD // 2 - 1) as i:
            for t in range(2):
                down(i, t)
        for t in range(2):
            down(KD // 2 - 1, t, more=False)
        dve.wait_ge(S["o_rstd"], 1)
        for k in range(KD):
            dve.scalar_tensor_tensor(out=x1[:, k, :], in0=x1[:, k, :], scalar=vec[:, V_FIN + k:V_FIN + k + 1],
                                     in1=f_rs[:], op0=ALU.mult, op1=ALU.mult).then_inc(S["o_fin"], 1)

    ctx.close()


def lay_out(inputs):
    f = {k: np.asarray(v) for k, v in inputs.items()}
    w_in = f["w_in"][0]

    def slabs(w):
        k, n = w.shape
        return np.ascontiguousarray(w.reshape(k // P, P, n).transpose(1, 0, 2)).reshape(P, -1)

    c = np.cumsum([0, 256, 256, 512, 512, 4, 4, 512, 512, 512, 512, 1024, 8, 512, 512, 512, 4096])
    (aq, ak, av, ao, ai, af, bb, bc, bx, cz, cx, cdt, sq, sk, sv, gt) = [w_in[:, c[n]:c[n + 1]] for n in range(16)]
    stream = np.zeros((N_STREAM, P, 1024), np.float32)

    def put(u, w, width=P):
        for n in range(w.shape[1] // width):
            stream[u + n] = slabs(w[:, n * width:(n + 1) * width])

    def put_tokens(u, w):
        for n in range(2):
            s = slabs(w[:, 256 * n:256 * n + 256])
            stream[u + 2 * n], stream[u + 2 * n + 1] = s[:, :1024], s[:, 1024:]

    put(U_DQ, sq); put(U_DK, sk); put_tokens(U_DV, sv)
    small = np.zeros((D, 96), np.float32)
    small[:, 0:4], small[:, 32:36], small[:, 64:72] = ai, af, cdt
    stream[U_SMALL, :, 0:KD * 96] = slabs(small)
    put(U_AQ, aq); put(U_AK, ak); put_tokens(U_AV, av); put(U_AO, ao)
    put(U_Z, cz); put(U_XBC, cx)
    for n in range(4):
        for q, w in enumerate((bc, bx, bb)):
            stream[U_B + 3 * n + q] = slabs(w[:, n * P:n * P + P])
    lift = f["w_lift"][0]
    for u0, b in ((U_GL_D, 3), (U_GL_A, 0), (U_GL_B, 1), (U_GL_C, 2)):
        for t in range(4):
            for q in range(2):
                d0 = P * (2 * t + q)
                stream[u0 + 3 * t + q] = slabs(gt[:, D * b + d0:D * b + d0 + P])
                stream[u0 + 3 * t + 2, :, 512 * q:512 * q + 512] = slabs(lift[b][:, d0:d0 + P])
    put(U_OUT, f["w_out"][0])
    up = f["w_up"][0]
    for t in range(NFF):
        for q in range(2):
            stream[U_UP + 2 * t + q] = slabs(up[:, FF * q + P * t:FF * q + P * t + P])
    down = np.zeros((4 * KD, P, 6 * P), np.float32)
    wd = f["w_down"][0]
    for t in range(KD):
        for q in range(4):
            k0, n = DOWN_K0[q], DOWN_K[q]
            down[4 * t + q, :, 0:n * P] = slabs(wd[k0 * P:(k0 + n) * P, t * P:t * P + P])

    def cols(v):
        v = v.reshape(-1, v.shape[-1] // P, P)
        return v.transpose(2, 1, 0)
    vec = np.zeros((P, N_VEC), np.float32)
    vec[:, V_MIX:V_MIX + 8] = cols(f["mix_norm_g"])[:, :, 0]
    vec[:, V_FFN:V_FFN + 8] = cols(f["ffn_norm_g"])[:, :, 0]
    vec[:, V_FIN:V_FIN + 8] = cols(f["final_norm_g"])[:, :, 0]
    vec[:, V_AG:V_AG + 4] = cols(f["a_norm_g"])[:, :, 0]
    vec[:, V_BCW:V_BCW + 12] = cols(f["b_conv_w"][0]).reshape(P, 12)
    vec[:, V_CCW:V_CCW + 32] = cols(f["c_conv_w"][0]).reshape(P, 32)
    vec[:, V_CCB:V_CCB + 8] = cols(f["c_conv_b"])[:, :, 0]
    vec[:, V_CNG:V_CNG + 4] = cols(f["c_norm_g"])[:, :, 0]
    vec[:, V_DSK:V_DSK + 4] = cols(np.repeat(f["c_d_skip"], 64, axis=1))[:, :, 0]
    fc = np.zeros((P, NFF, 2, 4), np.float32)
    fc[:, :, :, 0:3] = cols(f["ffn_conv_w"][0]).reshape(P, 2, NFF, 3).transpose(0, 2, 1, 3)
    fc[:, :, :, 3] = cols(f["ffn_conv_b"]).reshape(P, 2, NFF).transpose(0, 2, 1)
    vec[:, V_FCW:] = fc.reshape(P, -1)
    rows = np.zeros((40, 4), np.float32)
    rows[0:4, 0] = f["a_igate_b"][0]
    rows[0:4, 1] = f["a_fgate_b"][0]
    rows[32:40, 1] = f["c_dt_bias"][0]
    rows[32:40, 2] = f["c_a_log"][0]
    xT = np.ascontiguousarray(f["x"][0].reshape(T, KD, P).transpose(2, 1, 0))
    return {"w_stream": stream, "w_down": down, "xT": xT, "vecs": vec, "rowsm": rows}


def kernel(**inputs):
    import concourse.bacc as bacc
    from concourse.bass_utils import run_bass_kernel_spmd

    nc = bacc.Bacc("TRN2", target_bir_lowering=False, num_devices=1)
    arrays = lay_out(inputs)
    aps = [nc.dram_tensor(n, a.shape, mybir.dt.from_np(a.dtype), kind="ExternalInput").ap()
           for n, a in arrays.items()]
    out = nc.dram_tensor("outT", (P, KD, T), F32, kind="ExternalOutput").ap()
    build(nc, *aps, out)
    r = run_bass_kernel_spmd(nc, [arrays], core_ids=[0])
    got = r.results[0]["outT"]
    return np.ascontiguousarray(got.transpose(2, 1, 0)).reshape(1, T, D)
```

```python
from contextlib import ExitStack

import numpy as np
import concourse.bass as bass
from concourse import mybir

ALU = mybir.AluOpType
ACT = mybir.ActivationFunctionType
F32 = mybir.dt.float32
F32R = mybir.dt.float32r

P = 128
T = 512
D = 1024
KD = D // P
FF = 2816
NFF = FF // P
NB = T // P
BLK_W = [T - P * j for j in range(NB)]
BLK_O = [sum(BLK_W[:j]) for j in range(NB)]
PACK = sum(BLK_W)
EPS = 1e-6
NEG = -1e30
A_HEADS, C_HEADS, D_HEADS = 4, 8, 4
A_SCALE = 64 ** -0.5
D_SCALE = 128 ** -0.5

U_DQ, U_DK, U_DV = 0, 4, 8
U_SMALL = 12
U_AQ, U_AK, U_AV, U_AO = 13, 15, 17, 21
U_XBC, U_GL_D, U_Z, U_B = 25, 33, 45, 49
U_GL_A, U_GL_B, U_GL_C = 61, 73, 85
U_OUT = 97
U_UP = U_OUT + KD
U_DOWN = U_UP + 2 * NFF
N_STREAM = U_DOWN
DOWN_K = [6, 6, 5, 5]
DOWN_K0 = [0, 6, 12, 17]
N_UNITS = U_DOWN + 4 * KD
RING = 4
GL = {U_GL_D: 0, U_GL_A: 1, U_GL_B: 0, U_GL_C: 1}
D_AT = [12 + 4 * h for h in range(D_HEADS)]
A_AT = [33 + 4 * h for h in range(A_HEADS)]
C_T = 52
C_AT = [C_T + 2 + 5 * (h // 2) + 2 * (h % 2) for h in range(C_HEADS)]
C_Y = [C_AT[2 * p + 1] + 2 for p in range(4)]
C_SQ = C_Y[3] + 2

V_MIX, V_FFN, V_FIN, V_AG = 0, 8, 16, 24
V_BCW, V_CCW, V_CCB, V_CNG, V_DSK = 28, 40, 72, 80, 84
V_FCW = 88
N_VEC = V_FCW + 4 * 2 * NFF


def front_tiles():
    made = {}
    for u in range(U_OUT):
        n, who = 1, "dve"
        if u in (U_DV, U_DV + 2, U_AV, U_AV + 2):
            n = 0
        elif u in (U_DV + 1, U_DV + 3, U_AV + 1, U_AV + 3):
            n = 2
        elif U_AO <= u < U_AO + 4 or U_Z <= u < U_Z + 4:
            who = "act"
        for g in GL:
            if g <= u < g + 12:
                n, who = (2, "dve") if (u - g) % 3 == 2 else (1, "act")
        made[u] = (n, who)
    return made


def build(nc, w_stream, w_down, xT, vecs, rowsm, outT):
    made = front_tiles()
    first_tile, order = {}, []
    counts = {"dve": 0, "act": 0}
    for u in range(U_OUT):
        first_tile[u] = len(order)
        n, who = made[u]
        for _ in range(n):
            counts[who] += 1
            order.append((who, counts[who]))
    PEEL = 4
    for u in range(U_OUT, U_UP + PEEL):
        first_tile[u] = len(order)
        counts["dve"] += 1
        order.append(("dve", counts["dve"]))
    TILES0, DVE0 = len(order), counts["dve"]
    BANK0 = 3 - first_tile[U_OUT]
    bank_of = [o % 4 if o < 12 else o % 3 if o < first_tile[U_OUT] else (o + BANK0) % 4 for o in range(TILES0)]

    UPS = 2 * NFF - PEEL
    DOWN_READ = DVE0 + UPS
    DOWN_BANK = [(TILES0 + BANK0 + q) % 4 for q in range(2)]

    TH = T // 2

    def toks(e):
        return slice(e * TH, e * TH + TH)

    def gb(o):
        return GB[bank_of[o]]

    ctx = ExitStack()
    base = 16512

    def at(name, shape, dt, offset):
        return nc.alloc_sbuf_tensor_at(name, shape, dt, offset=offset)

    class Map:

        def __init__(self, offset):
            self.at = offset

        def put(self, name, shape, dt=F32):
            size = 4 * int(np.prod(shape[1:]))
            t = at(name, shape, dt, self.at)
            self.at += (size + 31) // 32 * 32
            return t

    m = Map(base)
    raw = m.put("raw", [P, RING, 1024])
    w_hi = m.put("w_hi", [P, RING, 1024], F32R)
    w_lo = m.put("w_lo", [P, RING, 1024], F32R)
    xn_hi = m.put("xn_hi", [P, KD, T], F32R)
    xn_lo = m.put("xn_lo", [P, KD, T], F32R)
    ones = m.put("ones", [P, P])
    ident = m.put("ident", [P, P])
    tri = m.put("tri", [P, P])
    tri_r = m.put("tri_r", [P, P], F32R)
    ones_r = m.put("ones_r", [P, P], F32R)
    causal = m.put("causal", [P, P])
    colT = m.put("colT", [P, NB, P])
    vec = m.put("vec", [P, N_VEC])
    fcw = vec[:, V_FCW:N_VEC].rearrange("p (t c) -> p t c", c=4)
    fin_g = vec[:, V_FIN:V_FIN + KD].rearrange("p (k one) -> p k one", one=1)
    rsm = m.put("rsm", [40, 4])
    cst = m.put("cst", [P, 4])
    END_CONST = m.at
    y_hi0 = m.put("y_hi0", [P, 4, T], F32R)
    y_lo0 = m.put("y_lo0", [P, 4, T], F32R)
    G0 = m.at
    merged = m.put("merged", [P, KD, T])
    gate = m.put("gate", [P, 2, T])
    m.at = G0 + 3 * 4 * 4 * T
    t0 = m.put("t0", [P, PACK])
    sp_lo = at("sp_lo", [P, PACK], F32R, m.at)
    t1 = m.put("t1", [P, PACK])
    A0 = m.at
    ak = m.put("ak", [P, 2, T])
    av = m.put("av", [P, NB, T])
    ao = m.put("ao", [P, 4, T])
    C0 = m.at
    zy = m.put("zy", [P, 4, T])
    xbc = m.put("xbc", [P, 8, T])
    stg = m.put("stg", [P, 2, T])
    nmb = m.put("nmb", [P, T])
    enb = m.put("enb", [P, T])
    Y1 = m.at
    y_hi1 = m.put("y_hi1", [P, 4, T], F32R)
    y_lo1 = m.put("y_lo1", [P, 4, T], F32R)
    assert m.at <= 229344, m.at
    y_hi, y_lo = (y_hi0, y_hi1), (y_lo0, y_lo1)
    g = Map(G0)
    dq, dk, dv = (g.put(n, [P, 4, T]) for n in ("dq", "dk", "dv"))
    x_in = at("x_in", [P, KD, T], F32, C0 + 4 * 4 * T)
    aq = at("aq", [P, A_HEADS, T], F32, C0)
    g = Map(Y1)
    negm = g.put("negm", [P, T])
    g_sp = g.put("g_sp", [40, T])
    g_ab = g.put("g_ab", [40, T])
    g_x = g.put("g_x", [40, T])
    g_row = g.put("g_row", [P, T])
    g_nm = g.put("g_nm", [4, 2, T])
    g_i = g.put("g_i", [4, T])
    g = Map(C0 + 4 * 4 * T)
    a_run = g.put("a_run", [40, PACK])
    g_one = g.put("g_one", [40, T])
    g_b = g.put("g_b", [40, T])
    sp_hi = g.put("sp_hi", [P, PACK], F32R)
    assert g.at <= C0 + 12 * 4 * T
    g = Map(A0)
    xdt = g.put("xdt", [P, NB, T])
    cbm = g.put("cbm", [P, PACK])
    abc = g.put("abc", [P, PACK])
    assert g.at <= C0
    g = Map(G0)
    f_cv = g.put("f_cv", [P, 2, 2, T])
    f_si = g.put("f_si", [P, T])
    f_sq = g.put("f_sq", [P, T])
    f_ac = g.put("f_ac", [P, T])
    f_rs = g.put("f_rs", [P, T])
    h_hi = g.put("h_hi", [P, NFF, T], F32R)
    h_lo = g.put("h_lo", [P, NFF, T], F32R)
    assert g.at <= 229344
    x1 = at("x1", [P, KD, T], F32, C0 + 5 * 4 * T)
    assert C0 + 5 * 4 * T >= G0 + 4 * T * (8 + NFF + 2) and Y1 >= C0 + 13 * 4 * T
    x_n2 = at("x_n2", [P, KD, T], F32, A0)
    assert G0 + 4 * T * (8 + 2) <= A0 and A0 + 4 * T * KD <= C0
    x2 = at("x2", [P, KD, T], F32, base + 3 * RING * 4096)

    GB = [ctx.enter_context(nc.psum_tensor(f"gb{i}", [P, T], F32)) for i in range(4)]
    X = [ctx.enter_context(nc.psum_tensor(f"xb{i}", [P, T], F32)) for i in range(4)]
    O_LAST, O_SUM = (GB[DOWN_BANK[1]], X[1]), (X[0], X[2])
    scr = nc.dram_tensor("scr_rows", [8, T], F32).ap()
    scr_x = nc.dram_tensor("scr_x", [P, KD, T], F32).ap()
    scr_a = nc.dram_tensor("scr_a", [8, PACK], F32).ap()

    names = """raw0 raw1 raw2 raw3 x0 x1 x2 x3 x4 x5 x6 x7 vec_loaded rsm_loaded built filled masks masks_r
        hi_ready lo_ready unit_done psum_read_dve psum_read_act act_own dve_own
        xg_hi xg_ready n1_sqr n1_acc n1_sum n1_rstd n1_xn n1_hi xn_ready
        merged_put merged_hi merged_ready
        d_scores d_masked d_soft_in d_soft d_sp_hi d_sp_lo d_suffix d_expo d_weights d_out d_hi d_lo
        g_log g_rows g_en g_trans g_cols rows_out a_out
        a_nm a_en a_arg a_dec a_scores a_w a_wsum a_numden a_h a_sq a_sum a_rstd a_y a_hi a_lo
        b_hi b_lo x_tap z_made
        c_trans c_xdt c_cb c_cbm c_abc c_arg c_dec c_w c_y c_z c_sq c_acc c_sum c_rstd c_fin c_hi c_lo
        x_again x1_out x1_back wo_hi wo_xg_ready wo_sq wo_acc n2_sum n2_rstd n2_xn n2_hi n2_ready
        f_tap f_tap1 f_conv f_silu f_h f_hi f_lo o_sq o_gain o_acc o_last o_sum o_rstd o_fin o_fin_pool
        out_stored""".split()
    S = {n: ctx.enter_context(nc.semaphore(n)) for n in names}
    block = ctx.enter_context(nc.Block())

    FIN_POOL = (2, 5, 7)
    FIN_DVE = (0, 1, 3, 4, 6)

    def gain(v, k):
        return vec[:, v + k:v + k + 1]

    def mg(k):
        return (y_hi0[:, k, :], y_lo0[:, k, :]) if k < 4 else (xn_hi[:, k, :], xn_lo[:, k, :])

    def x1g(k):
        return (xn_hi[:, k, :], xn_lo[:, k, :]) if k < 4 else (y_hi1[:, k - 4, :], y_lo1[:, k - 4, :])

    def merged_at(s):
        return {U_GL_C + 4: (0, 1), U_GL_C + 7: (2, 3), U_OUT - 1: (4, 5), U_OUT: (6, 7)}.get(s, ())

    N2_AT = {1: (0, 1, 2), 2: (3, 4, 5, 6, 7), 3: ()}

    def blk(j):
        return slice(BLK_O[j], BLK_O[j] + BLK_W[j])

    def diag(j):
        return slice(BLK_O[j], BLK_O[j] + P)

    @block.sync
    def _(sp):
        for k in range(KD):
            sp.dma_start(x_in[:, k, :], xT[:, k, :]).then_inc(S[f"x{k}"], 16)
            for r in {0: (0, 1), KD - 1: (2, 3)}.get(k, ()):
                sp.dma_start(raw[:, r, :], w_stream[r]).then_inc(S[f"raw{r}"], 16)
        with sp.Fori(1, U_DOWN // RING) as i:
            for r in range(RING):
                sp.wait_ge(S["lo_ready"], RING * i - RING + r + 1)
                sp.dma_start(raw[:, r, :], w_stream[RING * i + r]).then_inc(S[f"raw{r}"], 16)
        r = 0
        sp.wait_ge(S["lo_ready"], U_DOWN - RING)
        sp.dma_start(raw[:, r, :], w_stream[U_DOWN - 1]).then_inc(S[f"raw{r}"], 16)
        for q in range(4 * KD):
            u = U_DOWN + q
            sp.wait_ge(S["lo_ready"], u - RING + 1)
            n = DOWN_K[q % 4] * P
            sp.dma_start(raw[:, u % RING, 0:n], w_down[q][:, 0:n]).then_inc(S[f"raw{u % RING}"], 16)
        for e in range(2):
            for k in range(KD):
                if k in FIN_POOL:
                    sp.wait_ge(S["o_fin_pool"], len(FIN_POOL) * e + FIN_POOL.index(k) + 1)
                else:
                    sp.wait_ge(S["o_fin"], len(FIN_DVE) * e + FIN_DVE.index(k) + 1)
                sp.dma_start(outT[:, k, toks(e)], x2[:, k, toks(e)]).then_inc(S["out_stored"], 16)
        sp.wait_ge(S["out_stored"], 16 * 2 * KD)

    @block.gpsimd
    def _(pool):
        pool.dma_start(rsm[:], rowsm).then_inc(S["rsm_loaded"], 16)
        pool.memset(ones[:], 1.0).then_inc(S["built"], 1)
        pool.memset(cst[:, 0:1], 1.0).then_inc(S["built"], 1)
        pool.memset(cst[:, 1:2], EPS).then_inc(S["built"], 1)
        for k in range(KD):
            pool.wait_ge(S["n1_sqr"], k + 1)
            sq = (nmb, enb)[k % 2]
            if k == 0:
                ins = pool.tensor_copy(stg[:, 0, :], sq[:])
            else:
                ins = pool.tensor_tensor(stg[:, 0, :], stg[:, 0, :], sq[:], ALU.add)
            ins.then_inc(S["n1_acc"], 1)
            pool.wait_ge(S["n1_acc"], k + 1)
        pool.wait_ge(S["n1_rstd"], 1)
        for k in range(KD):
            pool.tensor_tensor(x_in[:, k, :], x_in[:, k, :], stg[:, 1, :], ALU.mult).then_inc(S["n1_xn"], 1)
        pool.memset(ident[:], 0.0).then_inc(S["filled"], 1)
        pool.memset(tri[:], 1.0).then_inc(S["filled"], 1)
        pool.memset(causal[:], 1.0).then_inc(S["filled"], 1)
        pool.wait_ge(S["filled"], 3)
        pool.affine_select(out=ident[:], in_=ident[:], compare_op=ALU.not_equal, fill=1.0, base=0,
                           pattern=[[-1, P]], channel_multiplier=1).then_inc(S["masks"], 1)
        pool.affine_select(out=tri[:], in_=tri[:], compare_op=ALU.is_ge, fill=0.0, base=0,
                           pattern=[[-1, P]], channel_multiplier=1).then_inc(S["masks"], 1)
        pool.affine_select(out=causal[:], in_=causal[:], compare_op=ALU.is_ge, fill=0.0, base=0,
                           pattern=[[1, P]], channel_multiplier=-1).then_inc(S["masks"], 1)
        pool.wait_ge(S["unit_done"], U_DV)
        pool.memset(negm[:], 0.0).then_inc(S["filled"], 1)
        pool.memset(g_x[:], 0.0).then_inc(S["masks"], 1)
        pool.memset(g_row[:], 0.0).then_inc(S["masks"], 1)
        for h in range(A_HEADS):
            z0 = 64 * (1 - h % 2)
            pool.wait_ge(S["masks"], 5 + h)
            pool.memset(aq[z0:z0 + 64, h, :], 0.0).then_inc(S["masks"], 1)
        pool.wait_ge(S["masks"], 9)
        pool.wait_ge(S["filled"], 4)
        pool.affine_select(out=negm[:], in_=negm[:], compare_op=ALU.is_ge, fill=NEG, base=-1,
                           pattern=[[1, T]], channel_multiplier=-1).then_inc(S["masks"], 1)
        pool.wait_ge(S["xn_ready"], KD)
        pool.memset(g_one[:], 1.0).then_inc(S["masks"], 1)
        pool.wait_ge(S["g_rows"], 1)
        pool.wait_ge(S["g_en"], 1)
        pool.dma_start(scr.rearrange("(w h) t -> h w t", h=4), g_nm[:, :, :]).then_inc(S["rows_out"], 16)
        pool.dma_start(scr_a, a_run[32:40, :]).then_inc(S["a_out"], 16)
        pool.wait_ge(S["rows_out"], 16)
        pool.wait_ge(S["a_out"], 16)
        for h in range(A_HEADS):
            if h:
                pool.wait_ge(S["a_arg"], 4 * h)
            pool.dma_start(nmb[:], scr[h:h + 1, :].to_broadcast([P, T])).then_inc(S["a_nm"], 16)
            if h:
                pool.wait_ge(S["a_h"], h)
            pool.dma_start(enb[:], scr[4 + h:5 + h, :].to_broadcast([P, T])).then_inc(S["a_en"], 16)
        for h in range(C_HEADS):
            if h:
                pool.wait_ge(S["c_arg"], 4 * h)
            else:
                pool.wait_ge(S["a_y"], 2 * A_HEADS)
            pool.dma_start(abc[:], scr_a[h:h + 1, :].to_broadcast([P, PACK])).then_inc(S["c_abc"], 16)
        pool.wait_ge(S["c_lo"], 4)
        pool.dma_start(x1[:], xT).then_inc(S["x_again"], 16)
        pool.wait_ge(S["psum_read_dve"], DVE0 - PEEL)
        pool.dma_start(scr_x, x1[:]).then_inc(S["x1_out"], 16)
        pool.wait_ge(S["n2_rstd"], 1)
        for k in range(KD):
            pool.tensor_tensor(x_n2[:, k, :], x1[:, k, :], f_rs[:], ALU.mult).then_inc(S["n2_xn"], 1)
        pool.wait_ge(S["x1_out"], 16)
        pool.wait_ge(S["unit_done"], U_DOWN)
        pool.dma_start(x2[:], scr_x).then_inc(S["x1_back"], 16)
        for e in range(2):
            pool.wait_ge(S["o_rstd"], e + 1)
            for k in FIN_POOL:
                pool.tensor_tensor(x2[:, k, toks(e)], x2[:, k, toks(e)], f_rs[:, toks(e)], ALU.mult)\
                    .then_inc(S["o_fin_pool"], 1)

    @block.tensor
    def _(pe):
        def gemm(out, r, c0, rhs, ks, kk0=0, kstep=1, first=True, last_=True):
            for n, k in enumerate(ks):
                lo, hi = c0 + n * P, c0 + n * P + P
                for q, (w, x) in enumerate(((w_hi, 0), (w_hi, 1), (w_lo, 0))):
                    ins = pe.matmul(out, w[:, r, lo:hi], rhs(k)[x], start=(first and n == 0 and q == 0),
                                    stop=(last_ and n == len(ks) - 1 and q == 2))
            return ins

        def xn(k):
            return xn_hi[:, k, :], xn_lo[:, k, :]

        def xg(k):
            return y_hi[k // 4][:, k % 4, :], y_lo[k // 4][:, k % 4, :]

        def bank_free(o):
            before = [p for p in range(o) if bank_of[p] == bank_of[o]]
            if before:
                who, n = order[before[-1]]
                pe.wait_ge(S[f"psum_read_{who}"], n)

        def unit(u):
            o = first_tile[u]
            n = made[u][0]
            pe.wait_ge(S["lo_ready"], u + 1)
            if U_DV <= u < U_DV + 4 or U_AV <= u < U_AV + 4:
                half = (u - (U_DV if u < U_DV + 4 else U_AV)) % 2
                for tb in range(NB):
                    if half == 0 and tb % 2 == 0:
                        bank_free(o + tb // 2)
                    out = gb(o + tb // 2)[:, 256 * (tb % 2):256 * (tb % 2) + 256]
                    for k in range(4):
                        c = k * 256
                        for q, (x, w) in enumerate(((xn_hi, w_hi), (xn_lo, w_hi), (xn_hi, w_lo))):
                            ins = pe.matmul(out, x[:, 4 * half + k, tb * P:tb * P + P], w[:, u % RING, c:c + 256],
                                            start=(half == 0 and k == 0 and q == 0 and tb % 2 == 0),
                                            stop=(half == 1 and k == 3 and q == 2), skip_group_check=True)
                ins.then_inc(S["unit_done"], 1)
                return
            for q in range(n):
                bank_free(o + q)
            gl = [g for g in GL if g <= u < g + 12]
            if gl and (u - gl[0]) % 3 == 2:
                s = GL[gl[0]]

                def yk(k):
                    return y_hi[s][:, k, :], y_lo[s][:, k, :]
                for q in range(2):
                    ins = gemm(gb(o + q)[:, :], u % RING, q * T, yk, range(4))
            elif u == U_SMALL:
                for k in range(KD):
                    for q, (w, x) in enumerate(((w_hi, 0), (w_hi, 1), (w_lo, 0))):
                        ins = pe.matmul(gb(o)[0:96, :], w[:, u % RING, 96 * k:96 * k + 96], xn(k)[x],
                                        start=(k == 0 and q == 0), stop=(k == KD - 1 and q == 2))
            else:
                ins = gemm(gb(o)[:, :], u % RING, 0, xg if u < U_DV else xn, range(KD))
            ins.then_inc(S["unit_done"], 1)

        pe.wait_ge(S["built"], 1)
        for _ in range(12):
            pe.matmul(X[3][:, 0:P], ones[:], ones[:], start=True, stop=True)
        for k in range(KD):
            pe.wait_ge(S["xg_ready"], k + 1)
            for u in (0, 1):
                if k == 0:
                    pe.wait_ge(S["lo_ready"], u + 1)
                ins = gemm(GB[u][:, :], u, k * P, xg, [k], first=(k == 0), last_=(k == KD - 1))
        ins.then_inc(S["unit_done"], 2)

        for u in range(U_OUT):
            for gfirst, need, cnt in ((U_GL_D, "d_lo", 4), (U_GL_A, "a_lo", 4), (U_GL_B, "b_lo", 4),
                                      (U_GL_C, "c_lo", 4)):
                if u == gfirst + 2:
                    pe.wait_ge(S[need], cnt)
            if u == U_DV:
                pe.wait_ge(S["xn_ready"], KD)
            if u >= 2:
                unit(u)
            if u == 2:
                pe.wait_ge(S["n1_acc"], KD)
                pe.wait_ge(S["built"], 3)
                pe.matmul(X[0][:, :], ones[:], stg[:, 0, :], start=True, stop=True).then_inc(S["n1_sum"], 1)
            if u == 22:
                pe.wait_ge(S["g_rows"], 1)
                pe.wait_ge(S["d_lo"], 2)
                for j in range(NB):
                    ins = pe.transpose(GB[3][:, j * P:j * P + P], g_row[:, j * P:j * P + P], ident[:])
                ins.then_inc(S["g_trans"], 1)
            if u in D_AT:
                h = D_AT.index(u)
                if h == 0:
                    pe.wait_ge(S["masks"], 10)
                    pe.wait_ge(S["psum_read_dve"], order[first_tile[U_SMALL] - 1][1])
                else:
                    pe.wait_ge(S["d_expo"], h)
                for j in range(NB):
                    ins = pe.matmul(X[j][:, 0:BLK_W[j]], dk[:, h, j * P:j * P + P], dq[:, h, j * P:T],
                                    start=True, stop=True)
                    ins.then_inc(S["d_scores"], 1)
            if u - 4 in D_AT:
                h = D_AT.index(u - 4)
                if h:
                    pe.wait_ge(S["d_lo"], h)
                if h == 2:
                    pe.wait_ge(S["g_cols"], 1)
                pe.wait_ge(S["d_weights"], h + 1)
                for j in range(NB):
                    ins = pe.matmul(GB[3][:, j * P:T], dv[:, j, h * P:h * P + P], t1[:, blk(j)],
                                    start=(j == 0), stop=(j == NB - 1), skip_group_check=True)
                ins.then_inc(S["d_out"], 1)
            if u - 3 in D_AT:
                h = D_AT.index(u - 3)
                if h == 0:
                    pe.wait_ge(S["masks_r"], 2)
                pe.wait_ge(S["d_sp_lo"], h + 1)
                for j in range(NB):
                    for jj in range(j, NB):
                        for part in (sp_hi, sp_lo):
                            ins = pe.matmul(X[j][:, P * (jj - j):BLK_W[j]], (tri_r if jj == j else ones_r)[:],
                                            part[:, blk(jj)], start=(jj == j and part is sp_hi),
                                            stop=(jj == NB - 1 and part is sp_lo), skip_group_check=True)
                    ins.then_inc(S["d_suffix"], 1)
            if u in A_AT:
                h = A_AT.index(u)
                if h == 0:
                    pe.wait_ge(S["d_expo"], 4)
                    pe.wait_ge(S["psum_read_dve"], order[first_tile[U_AO] - 1][1])
                else:
                    pe.wait_ge(S["a_h"], h)
                for j in range(NB):
                    ins = pe.matmul(X[j][:, 0:BLK_W[j]], ak[:, h // 2, j * P:j * P + P],
                                    aq[:, h, j * P:T], start=True, stop=True)
                    ins.then_inc(S["a_scores"], 1)
            if u - 2 in A_AT:
                h = A_AT.index(u - 2)
                pe.wait_ge(S["a_w"], h + 1)
                for j in range(NB):
                    pe.matmul(X[0][:, j * P:T], av[:, j, h * P:h * P + P], t0[:, blk(j)], start=(j == 0),
                              stop=(j == NB - 1), skip_group_check=True)
                pe.wait_ge(S["a_wsum"], h + 1)
                ins = pe.matmul(X[1][:, :], ones[:], stg[:, 0, :], start=True, stop=True)
                ins.then_inc(S["a_numden"], 1)
            if u - 4 in A_AT:
                h = A_AT.index(u - 4)
                pe.wait_ge(S["a_sq"], h + 1)
                if h == 0:
                    pe.wait_ge(S["d_lo"], 4)
                else:
                    pe.wait_ge(S["a_rstd"], h)
                pe.matmul(GB[3][:, :], ones[:], t1[:, T:2 * T], start=True, stop=True).then_inc(S["a_sum"], 1)
            if u == C_T:
                pe.wait_ge(S["z_made"], 8)
                pe.wait_ge(S["a_h"], 4)
                for b in range(NB):
                    for c in range(4):
                        ins = pe.transpose(X[b][:, c * P:c * P + P], xbc[:, c, b * P:b * P + P], ident[:])
                    ins.then_inc(S["c_trans"], 1)
            if u in (C_T + 1, C_Y[1] + 1):
                g = 0 if u == C_T + 1 else 1
                if g == 0:
                    pe.wait_ge(S["c_xdt"], 4)
                else:
                    pe.wait_ge(S["c_z"], 2)
                for j in range(NB):
                    ins = pe.matmul(X[j][:, 0:BLK_W[j]], xbc[:, 4 + g, j * P:j * P + P], xbc[:, 6 + g, j * P:T],
                                    start=True, stop=True)
                    ins.then_inc(S["c_cb"], 1)
            if u in C_Y:
                p = C_Y.index(u)
                pe.wait_ge(S["c_w"], 2 * p + 2)
                if p >= 2:
                    pe.wait_ge(S["c_z"], p - 1)
                for j in range(NB):
                    for q, tt in enumerate((t0, t1)):
                        h = 2 * p + q
                        ins = pe.matmul(X[p % 2][64 * q:64 * q + 64, j * P:T], xdt[:, j, h * 64:h * 64 + 64],
                                        tt[:, blk(j)], start=(j == 0), stop=(j == NB - 1), skip_group_check=True)
                ins.then_inc(S["c_y"], 1)
            if u == C_SQ + 2:
                pe.wait_ge(S["c_acc"], 1)
                pe.wait_ge(S["a_rstd"], 4)
                pe.matmul(GB[3][:, :], ones[:], t0[:, 0:T], start=True, stop=True).then_inc(S["c_sum"], 1)

        for u in range(U_OUT, U_UP):
            pe.wait_ge(S["lo_ready"], u + 1)
            bank_free(first_tile[u])
            for k in range(KD):
                if u == U_OUT:
                    pe.wait_ge(S["merged_ready"], k + 1)
                ins = gemm(gb(first_tile[u])[:, :], u % RING, k * P, mg, [k], first=(k == 0), last_=(k == KD - 1))
            ins.then_inc(S["unit_done"], 1)

        for u in range(U_UP, U_UP + PEEL):
            pe.wait_ge(S["lo_ready"], u + 1)
            bank_free(first_tile[u])
            for k in range(KD):
                if u == U_UP:
                    pe.wait_ge(S["wo_xg_ready"], k + 1)
                    if k == KD - 1:
                        pe.wait_ge(S["wo_acc"], KD)
                        pe.matmul(X[0][:, :], ones[:], f_ac[:], start=True, stop=True).then_inc(S["n2_sum"], 1)
                ins = gemm(gb(first_tile[u])[:, :], u % RING, k * P, x1g, [k], first=(k == 0), last_=(k == KD - 1))
            ins.then_inc(S["unit_done"], 1)

        with pe.Fori(0, UPS // 4) as i:
            for q in range(4):
                pe.wait_ge(S["lo_ready"], U_UP + PEEL + 4 * i + q + 1)
                pe.wait_ge(S["psum_read_dve"], DVE0 - 3 + 4 * i + q)
                for k in range(KD):
                    if q == 0:
                        pe.wait_ge(S["n2_ready"], k + 1)
                    ins = gemm(GB[(TILES0 + BANK0 + q) % 4][:, :], (U_UP + q) % RING, k * P, mg, [k], first=(k == 0),
                               last_=(k == KD - 1))
                ins.then_inc(S["unit_done"], 1)
        def hk(k):
            return h_hi[:, k, :], h_lo[:, k, :]

        def down(i, t):
            for q in range(4):
                pe.wait_ge(S["lo_ready"], U_DOWN + 8 * i + 4 * t + q + 1)
                if q == 0:
                    pe.wait_ge(S["psum_read_dve"], DOWN_READ - 1 + 2 * i + t)
                if t == 0:
                    pe.wait_ge(S["f_lo"], DOWN_K0[q] + DOWN_K[q])
                gemm(GB[DOWN_BANK[t]][:, :], (U_DOWN + q) % RING, 0, hk, range(DOWN_K0[q], DOWN_K0[q] + DOWN_K[q]),
                     first=(q == 0), last_=(q == 3)).then_inc(S["unit_done"], 1)
        with pe.Fori(0, KD // 2 - 1) as i:
            for t in range(2):
                down(i, t)
        down(KD // 2 - 1, 0)

        def last_sum(e):
            pe.wait_ge(S["o_acc"], KD - 1)
            pe.matmul(O_SUM[e][:, 0:TH], ones[:], f_ac[:, toks(e)], start=True, stop=False)
            pe.wait_ge(S["o_sq"], KD + e)
            pe.matmul(O_SUM[e][:, 0:TH], ones[:], f_sq[:, toks(e)], start=False, stop=True).then_inc(S["o_sum"], 1)
        for e in range(2):
            def hk_half(k):
                return h_hi[:, k, toks(e)], h_lo[:, k, toks(e)]
            for q in range(4):
                pe.wait_ge(S["lo_ready"], N_UNITS - 4 + q + 1)
                if e == 0 and q == 0:
                    pe.wait_ge(S["psum_read_dve"], DOWN_READ + KD - 2)
                ins = gemm(O_LAST[e][:, 0:TH], (U_DOWN + q) % RING, 0, hk_half,
                           range(DOWN_K0[q], DOWN_K0[q] + DOWN_K[q]), first=(q == 0), last_=(q == 3))
                if e == 1 and q == 0:
                    last_sum(0)
            ins.then_inc(S["o_last"], 1)
        last_sum(1)

    @block.scalar
    def _(act):
        own = [0]

        EXP_LN, SIGMOID, SILU = "natural_log_exp_and_others", "sigmoid_and_others", "silu_and_others"
        loaded = [None]

        def table(name):
            if loaded[0] != name:
                act.preload_act_table_set(name)
                loaded[0] = name

        def link(ins):
            own[0] = own[0] + 1
            ins.then_inc(S["act_own"], 1)
            act.wait_ge(S["act_own"], own[0])

        def hi(u, r, rep, n=1024):
            act.wait_ge(S[f"raw{r}"], 16 * rep + 16)
            act.activation(w_hi[:, r, 0:n], raw[:, r, 0:n], ACT.Copy).then_inc(S["hi_ready"], 1)

        def rstd(out, summed, n):
            table(EXP_LN)
            link(act.activation(out, summed, ACT.Ln, bias=cst[:, 1:2], scale=1.0 / n))
            return act.activation(out, out, ACT.Exp, scale=-0.5)

        act.dma_start(vec[:], vecs).then_inc(S["vec_loaded"], 16)
        table(EXP_LN)
        act.wait_ge(S["vec_loaded"], 16)

        def square(k):
            if k >= 2:
                act.wait_ge(S["n1_acc"], k - 1)
            act.activation((nmb, enb)[k % 2][:], x_in[:, k, :], ACT.Square).then_inc(S["n1_sqr"], 1)
        for k in range(KD):
            act.wait_ge(S[f"x{k}"], 16)
            act.activation(y_hi[k // 4][:, k % 4, :], x_in[:, k, :], ACT.Identity, scale=gain(V_MIX, k))\
                .then_inc(S["xg_hi"], 1)
            if k == 0:
                hi(0, 0, 0)
                hi(1, 1, 0)
            if k < 4:
                square(k)
        for r in (2, 3):
            hi(r, r, 0)
            square(2 * r)
            square(2 * r + 1)
        act.wait_ge(S["built"], 3)
        act.wait_ge(S["n1_sum"], 1)
        rstd(stg[:, 1, :], X[0][:, :], D).then_inc(S["n1_rstd"], 1)

        def evac(u):
            if made[u][0] == 0:
                return
            o = first_tile[u]
            ps = gb(o)
            if U_AO <= u < U_AO + 4:
                table(SIGMOID)
                act.activation(ao[:, u - U_AO, :], ps[:, :], ACT.Sigmoid).then_inc(S["psum_read_act"], 1)
            elif U_Z <= u < U_Z + 4:
                if u == U_Z:
                    act.wait_ge(S["a_scores"], NB * A_HEADS)
                table(SILU)
                act.activation(zy[:, u - U_Z, :], ps[:, :], ACT.Silu).then_inc(S["psum_read_act"], 1)
            elif U_XBC <= u < U_XBC + 8:
                c = u - U_XBC
                if c == 0:
                    act.wait_ge(S["a_out"], 16)
                    act.wait_ge(S["psum_read_dve"], order[first_tile[U_DV]][1])
                if c >= 2:
                    act.wait_ge(S["z_made"], c - 1)
                table(SILU)
                act.activation(stg[:, c % 2, :], ps[:, :], ACT.Identity, bias=vec[:, V_CCB + c:V_CCB + c + 1],
                               scale=vec[:, V_CCW + 4 * c + 3:V_CCW + 4 * c + 4]).then_inc(S["x_tap"], 1)
                for b in (c - 1, c) if c == 7 else (c - 1,) if c else ():
                    if b == 4:
                        act.wait_ge(S["d_suffix"], NB * D_HEADS)
                    act.wait_ge(S["psum_read_dve"], order[first_tile[U_XBC + b]][1])
                    act.activation(xbc[:, b, :], stg[:, b % 2, :], ACT.Silu).then_inc(S["z_made"], 1)
            for g in GL:
                if g <= u < g + 12 and (u - g) % 3 < 2:
                    n = list(GL).index(g) * 4 + (u - g) // 3
                    if n == 0:
                        act.wait_ge(S["d_lo"], 4)
                    q = (u - g) % 3
                    table(SIGMOID)
                    if 1 <= n < 5:
                        act.wait_ge(S["psum_read_dve"], order[first_tile[U_GL_D + 3 * (n - 1) + 2] + q][1])
                    elif n >= 5:
                        act.wait_ge(S["merged_put"], 2 * (n - 5) + q + 1)
                    act.activation(gate[:, q, :], ps[:, :], ACT.Sigmoid).then_inc(S["psum_read_act"], 1)

        for u in range(U_OUT):
            act.wait_ge(S["unit_done"], u + 1)
            hi(u + RING, u % RING, (u + RING) // RING)
            s = u + 1
            if s - 4 in D_AT:
                h = D_AT.index(s - 4)
                table(EXP_LN)
                act.wait_ge(S["d_expo"], h + 1)
                act.activation(t1[:], t0[:], ACT.Exp).then_inc(S["d_weights"], 1)
            evac(u)
            if 2 <= u < 2 + KD // 2:
                for k in (2 * u - 4, 2 * u - 3):
                    act.wait_ge(S["n1_xn"], k + 1)
                    act.activation(xn_hi[:, k, :], x_in[:, k, :], ACT.Identity, scale=gain(V_MIX, k))\
                        .then_inc(S["n1_hi"], 1)
            if s == 9:
                act.wait_ge(S["masks"], 3)
                act.activation(tri_r[:], tri[:], ACT.Copy).then_inc(S["masks_r"], 1)
                act.activation(ones_r[:], ones[:], ACT.Copy).then_inc(S["masks_r"], 1)
            if s - 5 in D_AT:
                h = D_AT.index(s - 5)
                act.wait_ge(S["d_out"], h + 1)
                act.activation(y_hi[0][:, h, :], GB[3][:, :], ACT.Copy).then_inc(S["d_hi"], 1)
            if s - 1 in D_AT:
                h = D_AT.index(s - 1)
                table(EXP_LN)
                act.wait_ge(S["d_masked"], h + 1)
                if h:
                    act.wait_ge(S["d_out"], h)
                link(act.activation(t1[:], t0[:], ACT.Abs))
                link(act.activation(t1[:], t1[:], ACT.Exp, scale=-1.0))
                act.activation(t1[:], t1[:], ACT.Ln, bias=cst[:, 0:1]).then_inc(S["d_soft_in"], 1)
            if s - 2 in D_AT:
                h = D_AT.index(s - 2)
                act.wait_ge(S["d_soft"], h + 1)
                act.activation(sp_hi[:], t1[:], ACT.Copy).then_inc(S["d_sp_hi"], 1)
            if s == 14:
                table(EXP_LN)
                act.wait_ge(S["psum_read_dve"], order[first_tile[U_SMALL]][1])
                link(act.activation(g_ab[:], g_x[:], ACT.Abs))
                link(act.activation(g_ab[:], g_ab[:], ACT.Exp, scale=-1.0))
                act.activation(g_ab[:], g_ab[:], ACT.Ln, bias=cst[0:40, 0:1]).then_inc(S["g_log"], 1)
                act.activation(rsm[32:40, 3:4], rsm[32:40, 2:3], ACT.Exp).then_inc(S["g_log"], 1)
            if s == 20:
                table(EXP_LN)
                act.wait_ge(S["g_rows"], 1)
                act.activation(g_nm[:, 1, :], g_nm[:, 1, :], ACT.Exp).then_inc(S["g_en"], 1)
            if s in A_AT:
                h = A_AT.index(s)
                table(EXP_LN)
                act.wait_ge(S["a_arg"], 4 * (h + 1))
                act.activation(t0[:], t0[:], ACT.Exp).then_inc(S["a_dec"], 1)
            if s - 4 in A_AT:
                h = A_AT.index(s - 4)
                act.wait_ge(S["a_h"], h + 1)
                act.activation(t1[:, T:2 * T], t1[:, 0:T], ACT.Square).then_inc(S["a_sq"], 1)
            if s - 5 in A_AT:
                h = A_AT.index(s - 5)
                table(EXP_LN)
                act.wait_ge(S["a_sum"], h + 1)
                link(act.activation(t1[:, T:2 * T], GB[3][:, :], ACT.Ln,
                                    bias=cst[:, 1:2], scale=1.0 / P))
                act.activation(t1[:, T:2 * T], t1[:, T:2 * T], ACT.Exp, scale=-0.5).then_inc(S["a_rstd"], 1)
            if s - 6 in A_AT:
                h = A_AT.index(s - 6)
                act.wait_ge(S["a_y"], 2 * h + 2)
                act.activation(y_hi[1][:, h, :], t1[:, 0:T], ACT.Copy).then_inc(S["a_hi"], 1)
            if U_B <= s - 1 < U_B + 12 and (s - 1 - U_B) % 3 == 2:
                c = (s - 1 - U_B) // 3
                act.wait_ge(S["psum_read_dve"], order[first_tile[U_B + 3 * c + 2]][1])
                if c == 0:
                    act.wait_ge(S["unit_done"], U_GL_D + 12)
                act.activation(y_hi[0][:, c, :], stg[:, 1, :], ACT.Copy).then_inc(S["b_hi"], 1)
            if s in C_AT:
                h = C_AT.index(s)
                table(EXP_LN)
                tt = (t0, t1)[h % 2]
                act.wait_ge(S["c_arg"], 4 * (h + 1))
                act.activation(tt[:], tt[:], ACT.Exp).then_inc(S["c_dec"], 1)
            if s == C_SQ:
                act.wait_ge(S["c_y"], C_HEADS // 2)
                act.wait_ge(S["c_fin"], 4)
                for c in range(4):
                    tt = (t0, t1)[c // 2]
                    act.activation(tt[:, (c % 2) * T:(c % 2) * T + T], zy[:, c, :], ACT.Square)\
                        .then_inc(S["c_sq"], 1)
            if s == C_SQ + 3:
                act.wait_ge(S["c_sum"], 1)
                rstd(t1[:, 0:T], GB[3][:, :], T).then_inc(S["c_rstd"], 1)
            if s == C_SQ + 5:
                act.wait_ge(S["unit_done"], U_GL_A + 12)
                for c in range(4):
                    act.wait_ge(S["c_fin"], 5 + c)
                    act.activation(y_hi[1][:, c, :], zy[:, c, :], ACT.Copy).then_inc(S["c_hi"], 1)
            for k in merged_at(s):
                act.wait_ge(S["merged_put"], 2 * KD + k + 1)
                act.activation(mg(k)[0], merged[:, k, :], ACT.Copy).then_inc(S["merged_hi"], 1)

        for k in range(KD):
            u = U_OUT + k
            act.wait_ge(S["unit_done"], u + 1)
            hi(u + RING, u % RING, (u + RING) // RING)
            act.wait_ge(S["psum_read_dve"], order[first_tile[u]][1])
            act.activation(x1g(k)[0], x1[:, k, :], ACT.Identity, scale=gain(V_FFN, k)).then_inc(S["wo_hi"], 1)
            if k:
                act.wait_ge(S["wo_acc"], k)
            act.activation(f_sq[:], x1[:, k, :], ACT.Square).then_inc(S["wo_sq"], 1)

        for q in range(PEEL):
            u = U_UP + q
            side, half = q % 2, q // 2
            if q:
                act.wait_ge(S["unit_done"], u + 1)
                hi(u + RING, u % RING, (u + RING) // RING)
            else:
                table(EXP_LN)
                act.wait_ge(S["n2_sum"], 1)
                rstd(f_rs[:], X[0][:, :], D).then_inc(S["n2_rstd"], 1)
                act.wait_ge(S["unit_done"], u + 1)
                hi(u + RING, u % RING, (u + RING) // RING)
                table(SILU)
            if q:
                for k in N2_AT[q]:
                    act.wait_ge(S["n2_xn"], k + 1)
                    if k == 4:
                        act.wait_ge(S["unit_done"], U_UP)
                    act.activation(mg(k)[0], x_n2[:, k, :], ACT.Identity, scale=gain(V_FFN, k))\
                        .then_inc(S["n2_hi"], 1)
            act.wait_ge(S["psum_read_dve"], order[first_tile[u]][1])
            act.activation(f_cv[:, half, side, :], f_sq[:], ACT.Identity, bias=fcw[:, q, 3:4],
                           scale=fcw[:, q, 2:3]).then_inc(S["f_tap"], 1)
            if side == 1:
                act.wait_ge(S["f_conv"], q)
                act.activation(f_si[:], f_cv[:, half, 0, :], ACT.Silu).then_inc(S["f_silu"], 1)
                act.wait_ge(S["f_h"], half + 1)
                act.activation(h_hi[:, half, :], f_cv[:, half, 1, :], ACT.Copy).then_inc(S["f_hi"], 1)

        def hi_loop(u, r, i, n=1024):
            act.wait_ge(S["unit_done"], u + 1)
            hi(0, r, i, n)

        with act.Fori(0, UPS // 4) as i:
            for q in range(4):
                side, half = q % 2, q // 2
                hi_loop(U_UP + PEEL + 4 * i + q, (U_UP + q) % RING, (U_UP + PEEL + q + RING) // RING + i)
                tile, pair = PEEL + 4 * i + q, PEEL // 2 + 2 * i + half
                act.activation(f_cv[:, half, side, :], GB[(TILES0 + BANK0 + q) % 4][:, :], ACT.Identity,
                               bias=fcw[:, tile, 3:4], scale=fcw[:, tile, 2:3]).then_inc(S["f_tap"], 1)
                if side == 1:
                    act.wait_ge(S["psum_read_dve"], DVE0 + 4 * i + q)
                    act.activation(f_si[:], f_cv[:, half, 0, :], ACT.Silu).then_inc(S["f_silu"], 1)
                    act.wait_ge(S["f_h"], pair + 1)
                    act.activation(h_hi[:, pair, :], f_cv[:, half, 1, :], ACT.Copy).then_inc(S["f_hi"], 1)

        def down(i, t):
            for q in range(4):
                hi_loop(U_DOWN + 8 * i + 4 * t + q, (U_DOWN + q) % RING,
                        (U_DOWN + q + RING) // RING + 2 * i + t, DOWN_K[q] * P)
            act.wait_ge(S["psum_read_dve"], DOWN_READ + 2 * i + t + 1)
            act.activation(f_sq[:], x2[:, 2 * i + t, :], ACT.Square).then_inc(S["o_sq"], 1)
            act.activation(x2[:, 2 * i + t, :], x2[:, 2 * i + t, :], ACT.Identity,
                           scale=fin_g[:, 2 * i + t, :]).then_inc(S["o_gain"], 1)
            act.wait_ge(S["o_acc"], 2 * i + t + 1)
        with act.Fori(0, KD // 2 - 1) as i:
            for t in range(2):
                down(i, t)
        table(EXP_LN)
        down(KD // 2 - 1, 0)
        for e in range(2):
            act.wait_ge(S["psum_read_dve"], DOWN_READ + KD + e)
            act.activation(f_sq[:, toks(e)], x2[:, KD - 1, toks(e)], ACT.Square).then_inc(S["o_sq"], 1)
            act.activation(x2[:, KD - 1, toks(e)], x2[:, KD - 1, toks(e)], ACT.Identity,
                           scale=fin_g[:, KD - 1, :]).then_inc(S["o_gain"], 1)
            act.wait_ge(S["o_sum"], e + 1)
            rstd(f_rs[:, toks(e)], O_SUM[e][:, 0:TH], D).then_inc(S["o_rstd"], 1)

    @block.vector
    def _(dve):
        own = [0]

        def link(ins):
            own[0] = own[0] + 1
            ins.then_inc(S["dve_own"], 1)
            dve.wait_ge(S["dve_own"], own[0])

        def lo(u, r, n=1024):
            dve.wait_ge(S["hi_ready"], u + 1)
            dve.tensor_tensor(w_lo[:, r, 0:n], raw[:, r, 0:n], w_hi[:, r, 0:n].bitcast(F32), ALU.subtract)\
                .then_inc(S["lo_ready"], 1)

        def split_lo(out, x, high):
            return dve.tensor_tensor(out, x, high.bitcast(F32), ALU.subtract)

        def split_gain(out, x, v, k, high):
            return dve.scalar_tensor_tensor(out=out, in0=x, scalar=gain(v, k), in1=high.bitcast(F32),
                                            op0=ALU.mult, op1=ALU.subtract)

        dve.wait_ge(S["vec_loaded"], 16)
        for k in range(KD):
            dve.wait_ge(S["xg_hi"], k + 1)
            split_gain(y_lo[k // 4][:, k % 4, :], x_in[:, k, :], V_MIX, k, y_hi[k // 4][:, k % 4, :])\
                .then_inc(S["xg_ready"], 1)
            if k == 0:
                lo(0, 0)
                lo(1, 1)
        for r in (2, 3):
            lo(r, r)

        def evac(u):
            n = made[u][0]
            if n == 0:
                return
            o = first_tile[u]
            ps = gb(o)

            def read(ins):
                ins.then_inc(S["psum_read_dve"], 1)
            if u < U_DK:
                if u == 0:
                    dve.wait_ge(S["n1_rstd"], 1)
                read(dve.scalar_tensor_tensor(out=dq[:, u, :], in0=ps[:, :], scalar=D_SCALE, in1=stg[:, 1, :],
                                              op0=ALU.mult, op1=ALU.mult))
            elif u < U_DV:
                read(dve.tensor_tensor(dk[:, u - U_DK, :], ps[:, :], stg[:, 1, :], ALU.mult))
            elif u < U_DV + 4 or U_AV <= u < U_AV + 4:
                dst, c = (dv, (u - U_DV) // 2) if u < U_DV + 4 else (av, (u - U_AV) // 2)
                for q in range(2):
                    read(dve.tensor_copy(dst[:, 2 * q:2 * q + 2, 256 * c:256 * c + 256],
                                         gb(o + q)[:, :].rearrange("p (b c) -> p b c", b=2)))
            elif u == U_SMALL:
                dve.wait_ge(S["masks"], 5)
                dve.wait_ge(S["rsm_loaded"], 16)
                link(dve.tensor_scalar(g_i[:], ps[0:4, :], rsm[0:4, 0:1], None, ALU.add))
                link(dve.tensor_scalar(g_x[0:4, :], ps[32:36, :], rsm[0:4, 1:2], -1.0, ALU.add, ALU.mult))
                dve.tensor_scalar(g_x[32:40, :], ps[64:72, :], rsm[32:40, 1:2], None, ALU.add)\
                    .then_inc(S["psum_read_dve"], 1)
            elif U_AQ <= u < U_AK:
                dve.wait_ge(S["masks"], 9)
                for q in range(2):
                    z0 = 64 * q
                    ins = dve.tensor_scalar(aq[z0:z0 + 64, 2 * (u - U_AQ) + q, :], ps[z0:z0 + 64, :], A_SCALE,
                                            None, ALU.mult)
                read(ins)
            elif U_AK <= u < U_AV:
                read(dve.tensor_copy(ak[:, u - U_AK, :], ps[:, :]))
            elif U_XBC <= u < U_XBC + 8:
                c = u - U_XBC
                w = stg[:, c % 2, :]
                dve.wait_ge(S["x_tap"], c + 1)
                for back in (1, 2, 3):
                    tap = V_CCW + 4 * c + 3 - back
                    ins = dve.scalar_tensor_tensor(out=w[:, back:T], in0=ps[:, 0:T - back],
                                                   scalar=vec[:, tap:tap + 1], in1=w[:, back:T],
                                                   op0=ALU.mult, op1=ALU.add)
                    if back < 3:
                        link(ins)
                read(ins)
            elif U_B <= u < U_B + 12:
                c, what = (u - U_B) // 3, (u - U_B) % 3
                if what == 0:
                    if c == 0:
                        dve.wait_ge(S["a_numden"], 4)
                    read(dve.tensor_copy(stg[:, 0, :], ps[:, :]))
                elif what == 1:
                    dve.wait_ge(S["psum_read_dve"], order[o - 1][1])
                    ins = dve.tensor_tensor(stg[:, 0, :], ps[:, :], stg[:, 0, :], ALU.mult)
                    read(ins)
                    dve.wait_ge(S["psum_read_dve"], order[o][1])
                    if c:
                        dve.wait_ge(S["b_hi"], c)
                    tap = V_BCW + 3 * c
                    link(dve.tensor_scalar(stg[:, 1, :], stg[:, 0, :], vec[:, tap + 2:tap + 3], None, ALU.mult))
                    for back in (1, 2):
                        link(dve.scalar_tensor_tensor(out=stg[:, 1, back:T], in0=stg[:, 0, 0:T - back],
                                                      scalar=vec[:, tap + 2 - back:tap + 3 - back],
                                                      in1=stg[:, 1, back:T], op0=ALU.mult, op1=ALU.add))
                else:
                    read(dve.tensor_tensor(stg[:, 1, :], ps[:, :], stg[:, 1, :], ALU.mult))
            for g in GL:
                if g <= u < g + 12 and (u - g) % 3 == 2:
                    b = list(GL).index(g)
                    t = (u - g) // 3
                    for q in range(2):
                        k = 2 * t + q
                        dve.wait_ge(S["psum_read_act"], order[o - 2 + q][1])
                        gt = gate[:, q, :]
                        ps = gb(o + q)
                        if b == 0:
                            dve.tensor_tensor(merged[:, k, :], ps[:, :], gt, ALU.mult)\
                                .then_inc(S["psum_read_dve"], 1)
                        else:
                            dve.tensor_tensor(gt, ps[:, :], gt, ALU.mult).then_inc(S["psum_read_dve"], 1)
                            dve.wait_ge(S["psum_read_dve"], order[o + q][1])
                            if b >= 2:
                                dve.wait_ge(S["merged_put"], KD * (b - 2) + k + 1)
                            dve.tensor_tensor(merged[:, k, :], merged[:, k, :], gt, ALU.add)\
                                .then_inc(S["merged_put"], 1)

        for u in range(U_OUT):
            if u < U_OUT - 1:
                lo(u + RING, u % RING)
            else:
                dve.wait_ge(S["unit_done"], u + 1)
            s = u + 1
            if s - 4 in D_AT:
                h = D_AT.index(s - 4)
                for j in range(NB):
                    dve.wait_ge(S["d_suffix"], NB * h + j + 1)
                    ins = dve.tensor_tensor(t0[:, blk(j)], t0[:, blk(j)], X[j][:, 0:BLK_W[j]], ALU.subtract)
                ins.then_inc(S["d_expo"], 1)
            evac(u)
            if 2 <= u < 2 + KD // 2:
                for k in (2 * u - 4, 2 * u - 3):
                    dve.wait_ge(S["n1_hi"], k + 1)
                    split_gain(xn_lo[:, k, :], x_in[:, k, :], V_MIX, k, xn_hi[:, k, :]).then_inc(S["xn_ready"], 1)
            if s - 1 in D_AT:
                h = D_AT.index(s - 1)
                if h == 0:
                    dve.wait_ge(S["masks"], 10)
                if h:
                    dve.wait_ge(S["d_weights"], h)
                for j in range(NB):
                    dve.wait_ge(S["d_scores"], NB * h + j + 1)
                    ins = dve.tensor_tensor(t0[:, blk(j)], X[j][:, 0:BLK_W[j]], negm[:, 0:BLK_W[j]], ALU.add)
                ins.then_inc(S["d_masked"], 1)
            if s - 2 in D_AT:
                h = D_AT.index(s - 2)
                dve.wait_ge(S["d_soft_in"], h + 1)
                dve.scalar_tensor_tensor(out=t1[:], in0=t0[:], scalar=0.0, in1=t1[:], op0=ALU.max,
                                         op1=ALU.add).then_inc(S["d_soft"], 1)
                dve.wait_ge(S["d_sp_hi"], h + 1)
                split_lo(sp_lo[:], t1[:], sp_hi[:]).then_inc(S["d_sp_lo"], 1)
            if s - 5 in D_AT:
                h = D_AT.index(s - 5)
                dve.wait_ge(S["d_hi"], h + 1)
                split_lo(y_lo[0][:, h, :], GB[3][:, :], y_hi[0][:, h, :]).then_inc(S["d_lo"], 1)
            if s == 15:
                dve.wait_ge(S["g_log"], 2)
                dve.wait_ge(S["masks"], 11)
                link(dve.scalar_tensor_tensor(out=g_sp[:], in0=g_x[:], scalar=0.0, in1=g_ab[:], op0=ALU.max,
                                              op1=ALU.add))
                link(dve.tensor_tensor_scan(g_b[0:4, :], g_one[0:4, :], g_sp[0:4, :], 0.0, ALU.mult, ALU.add))
            if s == 17:
                link(dve.tensor_tensor(g_row[0:4, :], g_i[:], g_b[0:4, :], ALU.add))
                link(dve.tensor_tensor_scan(g_i[:], g_row[0:4, :], g_row[0:4, :], 0.0, ALU.max, ALU.max))
                link(dve.tensor_scalar(g_b[32:40, :], g_sp[32:40, :], rsm[32:40, 3:4], -1.0, ALU.mult, ALU.mult))
                link(dve.tensor_scalar(g_nm[:, 0, :], g_i[:], -1.0, None, ALU.mult))
                link(dve.tensor_tensor(g_nm[:, 1, :], g_b[0:4, :], g_i[:], ALU.subtract))
                link(dve.tensor_copy(g_row[32:40, :], g_sp[32:40, :]))
            if s == 19:
                for j in range(NB):
                    link(dve.tensor_tensor_scan(a_run[32:40, blk(j)], g_one[32:40, 0:BLK_W[j]],
                                                g_b[32:40, j * P:T], 0.0, ALU.mult, ALU.add))
                for j in range(NB):
                    ins = dve.tensor_copy(g_row[64:72, j * P:j * P + P], a_run[32:40, diag(j)])
                    if j < NB - 1:
                        link(ins)
                ins.then_inc(S["g_rows"], 1)
            if s == 23:
                dve.wait_ge(S["g_trans"], 1)
                dve.tensor_copy(colT[:, :, :], GB[3][:, :].rearrange("p (b c) -> p b c", b=NB))\
                    .then_inc(S["g_cols"], 1)
                dve.wait_ge(S["g_cols"], 1)
            if s in A_AT:
                h = A_AT.index(s)
                dve.wait_ge(S["a_nm"], 16 * (h + 1))
                if h:
                    dve.wait_ge(S["a_numden"], h)
                else:
                    dve.wait_ge(S["d_weights"], 4)
                for j in range(NB):
                    dve.tensor_scalar(t0[:, blk(j)], nmb[:, j * P:T], colT[:, j, h:h + 1], 0.0, ALU.add,
                                      ALU.min).then_inc(S["a_arg"], 1)
            if s - 1 in A_AT:
                h = A_AT.index(s - 1)
                dve.wait_ge(S["a_dec"], h + 1)
                if h == 0:
                    dve.wait_ge(S["z_made"], 8)
                for j in range(NB):
                    dve.wait_ge(S["a_scores"], NB * h + j + 1)
                    ins = dve.tensor_tensor(t0[:, blk(j)], t0[:, blk(j)], X[j][:, 0:BLK_W[j]], ALU.mult)
                link(ins)
                for j in range(NB):
                    ins = dve.tensor_tensor(t0[:, diag(j)], t0[:, diag(j)], causal[:], ALU.mult)
                ins.then_inc(S["a_w"], 1)
                dve.wait_ge(S["a_w"], h + 1)
                link(dve.tensor_copy(stg[:, 0, 0:P], t0[:, 0:P]))
                link(dve.tensor_tensor(stg[:, 0, P:T], t0[:, P:T], t0[:, blk(1)], ALU.add))
                link(dve.tensor_tensor(stg[:, 0, 2 * P:T], stg[:, 0, 2 * P:T], t0[:, blk(2)], ALU.add))
                dve.tensor_tensor(stg[:, 0, 3 * P:T], stg[:, 0, 3 * P:T], t0[:, blk(3)], ALU.add)\
                    .then_inc(S["a_wsum"], 1)
            if s - 3 in A_AT:
                h = A_AT.index(s - 3)
                dve.wait_ge(S["a_numden"], h + 1)
                dve.wait_ge(S["a_en"], 16 * (h + 1))
                if h:
                    dve.wait_ge(S["a_lo"], h)
                else:
                    dve.wait_ge(S["d_out"], 4)
                link(dve.scalar_tensor_tensor(out=t1[:, T:2 * T], in0=X[1][:, :], scalar=-1.0, in1=enb[:],
                                              op0=ALU.mult, op1=ALU.max))
                link(dve.tensor_tensor(t1[:, T:2 * T], X[1][:, :], t1[:, T:2 * T], ALU.max))
                link(dve.reciprocal(t1[:, T:2 * T], t1[:, T:2 * T]))
                dve.tensor_tensor(t1[:, 0:T], X[0][:, :], t1[:, T:2 * T], ALU.mult).then_inc(S["a_h"], 1)
            if s - 5 in A_AT:
                h = A_AT.index(s - 5)
                dve.wait_ge(S["a_rstd"], h + 1)
                dve.wait_ge(S["psum_read_act"], order[first_tile[U_AO + 3]][1])
                dve.scalar_tensor_tensor(out=t1[:, 0:T], in0=t1[:, 0:T], scalar=vec[:, V_AG + h:V_AG + h + 1],
                                         in1=t1[:, T:2 * T], op0=ALU.mult, op1=ALU.mult).then_inc(S["a_y"], 1)
                dve.wait_ge(S["a_y"], 2 * h + 1)
                dve.tensor_tensor(t1[:, 0:T], t1[:, 0:T], ao[:, h, :], ALU.mult).then_inc(S["a_y"], 1)
            if s - 6 in A_AT:
                h = A_AT.index(s - 6)
                dve.wait_ge(S["a_hi"], h + 1)
                split_lo(y_lo[1][:, h, :], t1[:, 0:T], y_hi[1][:, h, :]).then_inc(S["a_lo"], 1)
            if U_B <= s - 1 < U_B + 12 and (s - 1 - U_B) % 3 == 2:
                c = (s - 1 - U_B) // 3
                dve.wait_ge(S["b_hi"], c + 1)
                split_lo(y_lo[0][:, c, :], stg[:, 1, :], y_hi[0][:, c, :]).then_inc(S["b_lo"], 1)
            if s - 1 == C_T:
                dve.wait_ge(S["a_lo"], 4)
                for b in range(NB):
                    dve.wait_ge(S["c_trans"], b + 1)
                    dve.tensor_tensor(xdt[:, b, :].rearrange("p (h c) -> p h c", h=C_HEADS),
                                      X[b][:, :].rearrange("p (h c) -> p h c", h=C_HEADS),
                                      colT[:, b, 32:40].unsqueeze(2).to_broadcast([P, C_HEADS, 64]),
                                      ALU.mult).then_inc(S["c_xdt"], 1)
            if s - 1 in (C_T + 1, C_Y[1] + 1):
                g = 0 if s - 1 == C_T + 1 else 1
                for j in range(NB):
                    dve.wait_ge(S["c_cb"], NB * g + j + 1)
                    dve.tensor_tensor(cbm[:, diag(j)], X[j][:, 0:P], causal[:], ALU.mult).then_inc(S["c_cbm"], 1)
                    if j < NB - 1:
                        dve.tensor_copy(cbm[:, BLK_O[j] + P:BLK_O[j] + BLK_W[j]], X[j][:, P:BLK_W[j]])\
                            .then_inc(S["dve_own"], 1)
                        own[0] += 1
            if s in C_AT:
                h = C_AT.index(s)
                tt = (t0, t1)[h % 2]
                dve.wait_ge(S["c_abc"], 16 * (h + 1))
                if h >= 2:
                    dve.wait_ge(S["c_y"], h // 2)
                for j in range(NB):
                    dve.tensor_scalar(tt[:, blk(j)], abc[:, blk(j)], colT[:, j, 64 + h:65 + h], 0.0,
                                      ALU.subtract, ALU.min).then_inc(S["c_arg"], 1)
            if s - 1 in C_AT:
                h = C_AT.index(s - 1)
                tt = (t0, t1)[h % 2]
                dve.wait_ge(S["c_dec"], h + 1)
                dve.wait_ge(S["dve_own"], own[0])
                dve.wait_ge(S["c_cbm"], NB * (h // 4 + 1))
                dve.tensor_tensor(tt[:], tt[:], cbm[:], ALU.mult).then_inc(S["c_w"], 1)
            if s - 1 in C_Y:
                p = C_Y.index(s - 1)
                dve.wait_ge(S["c_y"], p + 1)
                xs = xbc[:, p, :]
                if p == 0:
                    dve.wait_ge(S["z_made"], 8)
                    dve.wait_ge(S["psum_read_act"], order[first_tile[U_Z + 3]][1])
                dve.scalar_tensor_tensor(out=xs, in0=xs, scalar=vec[:, V_DSK + p:V_DSK + p + 1],
                                         in1=X[p % 2][:, :], op0=ALU.mult, op1=ALU.add).then_inc(S["c_z"], 1)
                dve.wait_ge(S["c_z"], p + 1)
                dve.tensor_tensor(zy[:, p, :], zy[:, p, :], xs, ALU.mult).then_inc(S["c_fin"], 1)
            if s == C_SQ + 1:
                dve.wait_ge(S["c_sq"], 4)
                link(dve.tensor_tensor(t0[:, 0:T], t0[:, 0:T], t0[:, T:2 * T], ALU.add))
                link(dve.tensor_tensor(t0[:, 0:T], t0[:, 0:T], t1[:, 0:T], ALU.add))
                dve.tensor_tensor(t0[:, 0:T], t0[:, 0:T], t1[:, T:2 * T], ALU.add).then_inc(S["c_acc"], 1)
            if s == C_SQ + 4:
                dve.wait_ge(S["c_rstd"], 1)
                dve.wait_ge(S["c_fin"], 4)
                for c in range(4):
                    dve.scalar_tensor_tensor(out=zy[:, c, :], in0=zy[:, c, :],
                                             scalar=vec[:, V_CNG + c:V_CNG + c + 1], in1=t1[:, 0:T],
                                             op0=ALU.mult, op1=ALU.mult).then_inc(S["c_fin"], 1)
            if s == C_SQ + 5:
                for c in range(4):
                    dve.wait_ge(S["c_hi"], c + 1)
                    split_lo(y_lo[1][:, c, :], zy[:, c, :], y_hi[1][:, c, :]).then_inc(S["c_lo"], 1)
            for k in merged_at(s):
                dve.wait_ge(S["merged_hi"], k + 1)
                split_lo(mg(k)[1], merged[:, k, :], mg(k)[0]).then_inc(S["merged_ready"], 1)
        lo(U_OUT - 1 + RING, (U_OUT - 1) % RING)

        dve.wait_ge(S["x_again"], 16)
        dve.wait_ge(S["merged_ready"], KD)
        link(dve.memset(f_ac[:], 0.0))
        for k in range(KD):
            u = U_OUT + k
            dve.wait_ge(S["unit_done"], u + 1)
            dve.tensor_tensor(x1[:, k, :], gb(first_tile[u])[:, :], x1[:, k, :], ALU.add)\
                .then_inc(S["psum_read_dve"], 1)
            dve.wait_ge(S["psum_read_dve"], order[first_tile[u]][1])
            dve.wait_ge(S["wo_hi"], k + 1)
            split_gain(x1g(k)[1], x1[:, k, :], V_FFN, k, x1g(k)[0]).then_inc(S["wo_xg_ready"], 1)
            dve.wait_ge(S["wo_sq"], k + 1)
            dve.tensor_tensor(f_ac[:], f_ac[:], f_sq[:], ALU.add).then_inc(S["wo_acc"], 1)
            dve.wait_ge(S["wo_acc"], k + 1)
            lo(u + RING, u % RING)

        for q in range(PEEL):
            u = U_UP + q
            side, half = q % 2, q // 2
            lo(u + RING, u % RING)
            if q:
                for k in N2_AT[q]:
                    dve.wait_ge(S["n2_hi"], k + 1)
                    split_gain(mg(k)[1], x_n2[:, k, :], V_FFN, k, mg(k)[0]).then_inc(S["n2_ready"], 1)
            if q == 0:
                dve.wait_ge(S["n2_rstd"], 1)
            else:
                dve.wait_ge(S["f_conv"], q)
            dve.tensor_tensor(f_sq[:], gb(first_tile[u])[:, :], f_rs[:], ALU.mult).then_inc(S["psum_read_dve"], 1)
            dve.wait_ge(S["psum_read_dve"], order[first_tile[u]][1])
            dve.wait_ge(S["f_tap"], q + 1)
            w = f_cv[:, half, side, :]
            dve.scalar_tensor_tensor(out=w[:, 1:T], in0=f_sq[:, 0:T - 1], scalar=fcw[:, q, 1:2],
                                     in1=w[:, 1:T], op0=ALU.mult, op1=ALU.add).then_inc(S["f_tap1"], 1)
            dve.wait_ge(S["f_tap1"], q + 1)
            dve.scalar_tensor_tensor(out=w[:, 2:T], in0=f_sq[:, 0:T - 2], scalar=fcw[:, q, 0:1],
                                     in1=w[:, 2:T], op0=ALU.mult, op1=ALU.add).then_inc(S["f_conv"], 1)
            if side == 1:
                dve.wait_ge(S["f_conv"], q + 1)
                dve.wait_ge(S["f_silu"], half + 1)
                dve.tensor_tensor(w, w, f_si[:], ALU.mult).then_inc(S["f_h"], 1)
                dve.wait_ge(S["f_hi"], half + 1)
                split_lo(h_lo[:, half, :], w, h_hi[:, half, :]).then_inc(S["f_lo"], 1)

        dve.wait_ge(S["x1_out"], 16)
        with dve.Fori(0, UPS // 4) as i:
            for q in range(4):
                side, half = q % 2, q // 2
                tile, pair = PEEL + 4 * i + q, PEEL // 2 + 2 * i + half
                lo(U_UP + PEEL + RING + 4 * i + q, (U_UP + q) % RING)
                dve.wait_ge(S["f_tap"], tile + 1)
                w, ps = f_cv[:, half, side, :], GB[(TILES0 + BANK0 + q) % 4]
                dve.scalar_tensor_tensor(out=w[:, 1:T], in0=ps[:, 0:T - 1], scalar=fcw[:, tile, 1:2],
                                         in1=w[:, 1:T], op0=ALU.mult, op1=ALU.add).then_inc(S["f_tap1"], 1)
                dve.wait_ge(S["f_tap1"], tile + 1)
                dve.scalar_tensor_tensor(out=w[:, 2:T], in0=ps[:, 0:T - 2], scalar=fcw[:, tile, 0:1],
                                         in1=w[:, 2:T], op0=ALU.mult, op1=ALU.add)\
                    .then_inc(S["psum_read_dve"], 1)
                if side == 1:
                    dve.wait_ge(S["psum_read_dve"], DVE0 + 4 * i + q + 1)
                    dve.wait_ge(S["f_silu"], pair + 1)
                    dve.tensor_tensor(w, w, f_si[:], ALU.mult).then_inc(S["f_h"], 1)
                    dve.wait_ge(S["f_hi"], pair + 1)
                    split_lo(h_lo[:, pair, :], w, h_hi[:, pair, :]).then_inc(S["f_lo"], 1)

        link(dve.memset(f_ac[:], 0.0))
        dve.wait_ge(S["x1_back"], 16)

        def down(i, t):
            k = 2 * i + t
            for q in range(4):
                lo(U_DOWN + RING + 4 * k + q, (U_DOWN + q) % RING, DOWN_K[q] * P)
            dve.wait_ge(S["unit_done"], U_DOWN + 4 * k + 4)
            dve.tensor_tensor(x2[:, k, :], GB[DOWN_BANK[t]][:, :], x2[:, k, :], ALU.add)\
                .then_inc(S["psum_read_dve"], 1)
            dve.wait_ge(S["o_sq"], k + 1)
            dve.tensor_tensor(f_ac[:], f_ac[:], f_sq[:], ALU.add).then_inc(S["o_acc"], 1)
            dve.wait_ge(S["o_acc"], k + 1)
        with dve.Fori(0, KD // 2 - 1) as i:
            for t in range(2):
                down(i, t)
        down(KD // 2 - 1, 0)
        for e in range(2):
            dve.wait_ge(S["o_last"], e + 1)
            dve.tensor_tensor(x2[:, KD - 1, toks(e)], O_LAST[e][:, 0:TH], x2[:, KD - 1, toks(e)], ALU.add)\
                .then_inc(S["psum_read_dve"], 1)
            dve.wait_ge(S["o_rstd"], e + 1)
            for k in FIN_DVE:
                dve.tensor_tensor(x2[:, k, toks(e)], x2[:, k, toks(e)], f_rs[:, toks(e)], ALU.mult)\
                    .then_inc(S["o_fin"], 1)

    ctx.close()


def lay_out(inputs):
    f = {k: np.asarray(v) for k, v in inputs.items()}
    w_in = f["w_in"][0]

    def slabs(w):
        k, n = w.shape
        return np.ascontiguousarray(w.reshape(k // P, P, n).transpose(1, 0, 2)).reshape(P, -1)

    c = np.cumsum([0, 256, 256, 512, 512, 4, 4, 512, 512, 512, 512, 1024, 8, 512, 512, 512, 4096])
    (aq, ak, av, ao, ai, af, bb, bc, bx, cz, cx, cdt, sq, sk, sv, gt) = [w_in[:, c[n]:c[n + 1]] for n in range(16)]
    stream = np.zeros((N_STREAM, P, 1024), np.float32)

    def put(u, w, width=P):
        for n in range(w.shape[1] // width):
            stream[u + n] = slabs(w[:, n * width:(n + 1) * width])

    def put_tokens(u, w):
        for n in range(2):
            s = slabs(w[:, 256 * n:256 * n + 256])
            stream[u + 2 * n], stream[u + 2 * n + 1] = s[:, :1024], s[:, 1024:]

    put(U_DQ, sq); put(U_DK, sk); put_tokens(U_DV, sv)
    small = np.zeros((D, 96), np.float32)
    small[:, 0:4], small[:, 32:36], small[:, 64:72] = ai, af, cdt
    stream[U_SMALL, :, 0:KD * 96] = slabs(small)
    put(U_AQ, aq); put(U_AK, ak); put_tokens(U_AV, av); put(U_AO, ao)
    put(U_Z, cz); put(U_XBC, cx)
    for n in range(4):
        for q, w in enumerate((bc, bx, bb)):
            stream[U_B + 3 * n + q] = slabs(w[:, n * P:n * P + P])
    lift = f["w_lift"][0]
    for u0, b in ((U_GL_D, 3), (U_GL_A, 0), (U_GL_B, 1), (U_GL_C, 2)):
        for t in range(4):
            for q in range(2):
                d0 = P * (2 * t + q)
                stream[u0 + 3 * t + q] = slabs(gt[:, D * b + d0:D * b + d0 + P])
                stream[u0 + 3 * t + 2, :, 512 * q:512 * q + 512] = slabs(lift[b][:, d0:d0 + P])
    put(U_OUT, f["w_out"][0])
    up = f["w_up"][0]
    for t in range(NFF):
        for q in range(2):
            stream[U_UP + 2 * t + q] = slabs(up[:, FF * q + P * t:FF * q + P * t + P])
    down = np.zeros((4 * KD, P, 6 * P), np.float32)
    wd = f["w_down"][0]
    for t in range(KD):
        for q in range(4):
            k0, n = DOWN_K0[q], DOWN_K[q]
            down[4 * t + q, :, 0:n * P] = slabs(wd[k0 * P:(k0 + n) * P, t * P:t * P + P])

    def cols(v):
        v = v.reshape(-1, v.shape[-1] // P, P)
        return v.transpose(2, 1, 0)
    vec = np.zeros((P, N_VEC), np.float32)
    vec[:, V_MIX:V_MIX + 8] = cols(f["mix_norm_g"])[:, :, 0]
    vec[:, V_FFN:V_FFN + 8] = cols(f["ffn_norm_g"])[:, :, 0]
    vec[:, V_FIN:V_FIN + 8] = cols(f["final_norm_g"])[:, :, 0]
    vec[:, V_AG:V_AG + 4] = cols(f["a_norm_g"])[:, :, 0]
    vec[:, V_BCW:V_BCW + 12] = cols(f["b_conv_w"][0]).reshape(P, 12)
    vec[:, V_CCW:V_CCW + 32] = cols(f["c_conv_w"][0]).reshape(P, 32)
    vec[:, V_CCB:V_CCB + 8] = cols(f["c_conv_b"])[:, :, 0]
    vec[:, V_CNG:V_CNG + 4] = cols(f["c_norm_g"])[:, :, 0]
    vec[:, V_DSK:V_DSK + 4] = cols(np.repeat(f["c_d_skip"], 64, axis=1))[:, :, 0]
    fc = np.zeros((P, NFF, 2, 4), np.float32)
    fc[:, :, :, 0:3] = cols(f["ffn_conv_w"][0]).reshape(P, 2, NFF, 3).transpose(0, 2, 1, 3)
    fc[:, :, :, 3] = cols(f["ffn_conv_b"]).reshape(P, 2, NFF).transpose(0, 2, 1)
    vec[:, V_FCW:] = fc.reshape(P, -1)
    rows = np.zeros((40, 4), np.float32)
    rows[0:4, 0] = f["a_igate_b"][0]
    rows[0:4, 1] = f["a_fgate_b"][0]
    rows[32:40, 1] = f["c_dt_bias"][0]
    rows[32:40, 2] = f["c_a_log"][0]
    xT = np.ascontiguousarray(f["x"][0].reshape(T, KD, P).transpose(2, 1, 0))
    return {"w_stream": stream, "w_down": down, "xT": xT, "vecs": vec, "rowsm": rows}


def kernel(**inputs):
    import concourse.bacc as bacc
    from concourse.bass_utils import run_bass_kernel_spmd

    nc = bacc.Bacc("TRN2", target_bir_lowering=False, num_devices=1)
    arrays = lay_out(inputs)
    aps = [nc.dram_tensor(n, a.shape, mybir.dt.from_np(a.dtype), kind="ExternalInput").ap()
           for n, a in arrays.items()]
    out = nc.dram_tensor("outT", (P, KD, T), F32, kind="ExternalOutput").ap()
    build(nc, *aps, out)
    r = run_bass_kernel_spmd(nc, [arrays], core_ids=[0])
    got = r.results[0]["outT"]
    return np.ascontiguousarray(got.transpose(2, 1, 0)).reshape(1, T, D)
```
